# Optimizing a Trainium2 kernel written in Bass

```python
import math
import jax, jax.numpy as jnp
from jax import lax
import numpy as np

D_MODEL = 1024
BATCH = 1
SEQ = 512
DEPTH = 2

A_HEADS = 8
A_HEAD_DIM = 64
A_V_DIM = 2 * A_HEAD_DIM
A_WIDTH = A_HEADS * A_V_DIM
B_HEADS = 8
B_QK_DIM = 64
B_V_DIM = 128
B_WIDTH = B_HEADS * B_V_DIM
CONV_WIDTH = 4
CHUNK = 64
Q_BLOCK = 128
ROPE_THETA = 10000.0
EPS = 1e-6
NEG_INIT = -1e30

SPLITS = (
    A_HEADS * 2 * A_HEAD_DIM,
    A_HEADS * 2 * A_HEAD_DIM,
    A_WIDTH,
    A_WIDTH,
    2 * B_HEADS * B_QK_DIM,
    B_WIDTH,
    B_HEADS,
    B_HEADS,
    B_WIDTH,
    B_WIDTH,
    D_MODEL,
    D_MODEL,
)
D_IN = sum(SPLITS)


def rmsnorm(x, g):
    xf = x.astype(jnp.float32)
    y = xf * lax.rsqrt(jnp.mean(xf * xf, axis=-1, keepdims=True) + EPS)
    return y.astype(x.dtype) * g

def rope(x, cos, sin):
    half = x.shape[-1] // 2
    x1, x2 = x[..., :half], x[..., half:]
    cos = cos.astype(x.dtype)
    sin = sin.astype(x.dtype)
    return jnp.concatenate([x1 * cos - x2 * sin, x2 * cos + x1 * sin], axis=-1)

def causal_conv(x, w, b):
    c = x.shape[-1]
    y = lax.conv_general_dilated(
        x, w[:, None, :].astype(x.dtype), window_strides=(1,), padding=[(CONV_WIDTH - 1, 0)],
        dimension_numbers=('NWC', 'WIO', 'NWC'), feature_group_count=c)
    return y + b

def diff_attention(q, k, v, lam):
    bsz, nh, s, _, dh = q.shape
    dv = v.shape[-1]
    nqb = s // Q_BLOCK
    scale = dh ** -0.5
    kpos = jnp.arange(s)

    def block(j):
        start = j * Q_BLOCK
        qb = lax.dynamic_slice_in_dim(q, start, Q_BLOCK, axis=2)
        sc = jnp.einsum('bhqrd,bhkrd->bhrqk', qb, k).astype(jnp.float32) * scale
        qpos = start + jnp.arange(Q_BLOCK)
        causal = kpos[None, :] <= qpos[:, None]
        p = jax.nn.softmax(jnp.where(causal, sc, -jnp.inf), axis=-1)
        a = p[:, :, 0] - lam * p[:, :, 1]
        return jnp.einsum('bhqk,bhkd->bhqd', a.astype(v.dtype), v)

    out = lax.map(block, jnp.arange(nqb))
    return jnp.transpose(out, (1, 2, 0, 3, 4)).reshape(bsz, nh, s, dv)

def mlstm_chunkwise(q, k, v, i_pre, f_pre):
    bsz, nh, s, dk = q.shape
    dv = v.shape[-1]
    nc = s // CHUNK
    f32 = jnp.float32
    q = q.astype(f32).reshape(bsz, nh, nc, CHUNK, dk) * (dk ** -0.5)
    k = k.astype(f32).reshape(bsz, nh, nc, CHUNK, dk)
    v = v.astype(f32).reshape(bsz, nh, nc, CHUNK, dv)
    ig = i_pre.astype(f32).reshape(bsz, nh, nc, CHUNK)
    b = jnp.cumsum(jax.nn.log_sigmoid(f_pre.astype(f32)).reshape(bsz, nh, nc, CHUNK), axis=-1)
    b_last = b[..., -1]
    w_log = b_last[..., None] - b + ig
    m_loc = jnp.max(w_log, axis=-1)
    wk = jnp.exp(w_log - m_loc[..., None])[..., None] * k
    c_loc = jnp.einsum('bhcld,bhcle->bhcde', wk, v)
    n_loc = jnp.sum(wk, axis=3)

    def step(carry, xs):
        c_st, n_st, m_st = carry
        bl, ml, cl, nl = xs
        m_new = jnp.maximum(bl + m_st, ml)
        a = jnp.exp(bl + m_st - m_new)
        e = jnp.exp(ml - m_new)
        c_new = a[..., None, None] * c_st + e[..., None, None] * cl
        n_new = a[..., None] * n_st + e[..., None] * nl
        return (c_new, n_new, m_new), (c_st, n_st, m_st)

    init = (jnp.zeros((bsz, nh, dk, dv), f32), jnp.zeros((bsz, nh, dk), f32), jnp.full((bsz, nh), NEG_INIT, f32))
    xs = (jnp.moveaxis(b_last, 2, 0), jnp.moveaxis(m_loc, 2, 0), jnp.moveaxis(c_loc, 2, 0), jnp.moveaxis(n_loc, 2, 0))
    _, (c_prev, n_prev, m_prev) = lax.scan(step, init, xs)
    c_prev = jnp.moveaxis(c_prev, 0, 2)
    n_prev = jnp.moveaxis(n_prev, 0, 2)
    m_prev = jnp.moveaxis(m_prev, 0, 2)
    causal = jnp.tril(jnp.ones((CHUNK, CHUNK), dtype=bool))
    d_log = jnp.where(causal, b[..., :, None] - b[..., None, :] + ig[..., None, :], -jnp.inf)
    inter_log = b + m_prev[..., None]
    m_t = jnp.maximum(inter_log, jnp.max(d_log, axis=-1))
    scores = jnp.einsum('bhctd,bhcsd->bhcts', q, k) * jnp.exp(d_log - m_t[..., None])
    inter_w = jnp.exp(inter_log - m_t)
    num = jnp.einsum('bhcts,bhcse->bhcte', scores, v) + inter_w[..., None] * jnp.einsum('bhctd,bhcde->bhcte', q, c_prev)
    den = jnp.sum(scores, axis=-1) + inter_w * jnp.einsum('bhctd,bhcd->bhct', q, n_prev)
    h = num / jnp.maximum(jnp.abs(den), jnp.exp(-m_t))[..., None]
    return h.reshape(bsz, nh, s, dv)

def hybrid_layer(x, cos, sin, layer_idx, norm_g, w_in, q_norm_g, k_norm_g, lambda_qk, attn_norm_g, w_out_a,
                 conv_w, conv_b, igate_b, fgate_b, mlstm_norm_g, w_out_b, w_o):
    bsz, s, _ = x.shape
    h = rmsnorm(x, norm_g)
    proj = h @ w_in
    idx = [int(i) for i in np.cumsum(SPLITS)[:-1]]
    aq, ak, av, az, bqk, bv, bi, bf, bo, bz, ga, gb = jnp.split(proj, idx, axis=-1)

    def two_map_heads(t):
        return t.reshape(bsz, s, A_HEADS, 2, A_HEAD_DIM).transpose(0, 2, 1, 3, 4)
    q = rope(rmsnorm(two_map_heads(aq), q_norm_g), cos, sin)
    k = rope(rmsnorm(two_map_heads(ak), k_norm_g), cos, sin)
    v = av.reshape(bsz, s, A_HEADS, A_V_DIM).transpose(0, 2, 1, 3)
    lam_init = 0.8 - 0.6 * math.exp(-0.3 * layer_idx)
    lq1, lk1, lq2, lk2 = lambda_qk[0], lambda_qk[1], lambda_qk[2], lambda_qk[3]
    lam = jnp.exp(jnp.sum(lq1 * lk1)) - jnp.exp(jnp.sum(lq2 * lk2)) + lam_init
    oa = diff_attention(q, k, v, lam)
    oa = rmsnorm(oa, attn_norm_g) * (1.0 - lam_init)
    oa = oa.transpose(0, 2, 1, 3).reshape(bsz, s, A_WIDTH) * jax.nn.silu(az)
    ya = oa @ w_out_a

    qk = jax.nn.silu(causal_conv(bqk, conv_w, conv_b))
    mq, mk = jnp.split(qk, 2, axis=-1)
    mq = mq.reshape(bsz, s, B_HEADS, B_QK_DIM).transpose(0, 2, 1, 3)
    mk = mk.reshape(bsz, s, B_HEADS, B_QK_DIM).transpose(0, 2, 1, 3)
    mv = bv.reshape(bsz, s, B_HEADS, B_V_DIM).transpose(0, 2, 1, 3)
    i_pre = (bi + igate_b).transpose(0, 2, 1)
    f_pre = (bf + fgate_b).transpose(0, 2, 1)
    hb = mlstm_chunkwise(mq, mk, mv, i_pre, f_pre).astype(x.dtype)
    hb = rmsnorm(hb, mlstm_norm_g).transpose(0, 2, 1, 3).reshape(bsz, s, B_WIDTH)
    hb = jax.nn.sigmoid(bo) * hb * jax.nn.silu(bz)
    yb = hb @ w_out_b

    u = jax.nn.sigmoid(ga) * ya + jax.nn.sigmoid(gb) * yb
    return x + u @ w_o

def first_inputs(seed: int = 0) -> dict:
    key = jax.random.key(seed)
    ks = jax.random.split(key, 16)
    f32 = jnp.float32
    x = jax.random.normal(ks[0], (BATCH, SEQ, D_MODEL), f32)
    offsets = jax.random.randint(ks[1], (BATCH, 1), 0, 4096, dtype=jnp.int32)
    positions = (offsets + jnp.arange(SEQ, dtype=jnp.int32)[None, :]).astype(jnp.int32)
    norm_g = 1.0 + 0.02 * jax.random.normal(ks[2], (DEPTH, D_MODEL), f32)
    w_in = jax.random.normal(ks[3], (DEPTH, D_MODEL, D_IN), f32) * D_MODEL ** -0.5
    q_norm_g = 1.0 + 0.02 * jax.random.normal(ks[4], (DEPTH, A_HEAD_DIM), f32)
    k_norm_g = 1.0 + 0.02 * jax.random.normal(ks[5], (DEPTH, A_HEAD_DIM), f32)
    lambda_qk = 0.1 * jax.random.normal(ks[6], (DEPTH, 4, A_HEAD_DIM), f32)
    attn_norm_g = 1.0 + 0.02 * jax.random.normal(ks[7], (DEPTH, A_V_DIM), f32)
    w_out_a = jax.random.normal(ks[8], (DEPTH, A_WIDTH, D_MODEL), f32) * A_WIDTH ** -0.5
    conv_w = jax.random.normal(ks[9], (DEPTH, CONV_WIDTH, 2 * B_HEADS * B_QK_DIM), f32) * CONV_WIDTH ** -0.5
    conv_b = 0.02 * jax.random.normal(ks[10], (DEPTH, 2 * B_HEADS * B_QK_DIM), f32)
    igate_b = 0.1 * jax.random.normal(ks[11], (DEPTH, B_HEADS), f32)
    fgate_b = jnp.linspace(3.0, 6.0, B_HEADS, dtype=f32)[None, :] + 0.1 * jax.random.normal(ks[12], (DEPTH, B_HEADS), f32)
    mlstm_norm_g = 1.0 + 0.02 * jax.random.normal(ks[13], (DEPTH, B_V_DIM), f32)
    w_out_b = jax.random.normal(ks[14], (DEPTH, B_WIDTH, D_MODEL), f32) * B_WIDTH ** -0.5
    w_o = jax.random.normal(ks[15], (DEPTH, D_MODEL, D_MODEL), f32) * D_MODEL ** -0.5
    return {'x': x, 'positions': positions, 'norm_g': norm_g, 'w_in': w_in, 'q_norm_g': q_norm_g,
            'k_norm_g': k_norm_g, 'lambda_qk': lambda_qk, 'attn_norm_g': attn_norm_g, 'w_out_a': w_out_a,
            'conv_w': conv_w, 'conv_b': conv_b, 'igate_b': igate_b, 'fgate_b': fgate_b,
            'mlstm_norm_g': mlstm_norm_g, 'w_out_b': w_out_b, 'w_o': w_o}

def first_block(x, positions, norm_g, w_in, q_norm_g, k_norm_g, lambda_qk, attn_norm_g, w_out_a,
              conv_w, conv_b, igate_b, fgate_b, mlstm_norm_g, w_out_b, w_o):
    inv_freq = ROPE_THETA ** (-jnp.arange(0, A_HEAD_DIM, 2, dtype=jnp.float32) / A_HEAD_DIM)
    ang = positions.astype(jnp.float32)[..., None] * inv_freq
    cos = jnp.cos(ang)[:, None, :, None, :]
    sin = jnp.sin(ang)[:, None, :, None, :]
    for l in range(DEPTH):
        x = hybrid_layer(x, cos, sin, l, norm_g[l], w_in[l], q_norm_g[l], k_norm_g[l], lambda_qk[l],
                         attn_norm_g[l], w_out_a[l], conv_w[l], conv_b[l], igate_b[l], fgate_b[l],
                         mlstm_norm_g[l], w_out_b[l], w_o[l])
    return x


RET_HEADS = 4
RET_QK_DIM = 128
RET_V_DIM = 256
RET_CHUNK = 128
SB_HEADS = 8
SB_HEAD_DIM = 128
SB_BLOCK = 128
D_FF = 4 * D_MODEL

ROPE_BASE = 10000.0
NORM_EPS = 1e-6
GN_EPS = 1e-5

RET_QK = RET_HEADS * RET_QK_DIM
RET_V = RET_HEADS * RET_V_DIM
SB_W = SB_HEADS * SB_HEAD_DIM
IN_SIZES = (RET_QK, RET_QK, RET_V, RET_V, SB_W, SB_W, SB_W, D_MODEL, D_MODEL)
D_IN_2 = RET_QK * 2 + RET_V * 2 + SB_W * 3 + D_MODEL * 2


def rmsnorm_2(x, gain):
    xf = x.astype(jnp.float32)
    y = xf * lax.rsqrt(jnp.mean(xf * xf, axis=-1, keepdims=True) + NORM_EPS)
    return (y * gain.astype(jnp.float32)).astype(x.dtype)

def rotary(t, pos):
    half = t.shape[-1] // 2
    inv_freq = ROPE_BASE ** (-jnp.arange(half, dtype=jnp.float32) / half)
    ang = pos.astype(jnp.float32)[:, None] * inv_freq[None, :]
    cos = jnp.cos(ang)[None, :, None, :]
    sin = jnp.sin(ang)[None, :, None, :]
    t1, t2 = t[..., :half], t[..., half:]
    return jnp.concatenate([t1 * cos - t2 * sin, t1 * sin + t2 * cos], axis=-1)

def retention(q, k, v, log_gamma):
    B, S, H, _ = q.shape
    C = RET_CHUNK
    N = S // C
    idx = jnp.arange(C, dtype=jnp.float32)
    diff = idx[:, None] - idx[None, :]
    decay = jnp.where(diff[None] >= 0,
                      jnp.exp(log_gamma[:, None, None] * jnp.maximum(diff, 0.0)[None]), 0.0)
    q_decay = jnp.exp(log_gamma[None, :] * (idx[:, None] + 1.0))
    k_decay = jnp.exp(log_gamma[None, :] * (C - 1.0 - idx[:, None]))
    chunk_decay = jnp.exp(log_gamma * C)

    def to_chunks(t):
        return t.reshape(B, N, C, H, t.shape[-1]).transpose(1, 0, 2, 3, 4)

    def step(state, qkv):
        qc, kc, vc = qkv
        scores = jnp.einsum('bchd,bshd->bhcs', qc, kc) * decay[None]
        inner = jnp.einsum('bhcs,bshe->bche', scores, vc)
        cross = jnp.einsum('bchd,bhde->bche', qc, state) * q_decay[None, :, :, None]
        state = state * chunk_decay[None, :, None, None] + jnp.einsum(
            'bshd,bshe->bhde', kc * k_decay[None, :, :, None], vc)
        return state, inner + cross

    init = jnp.zeros((B, H, q.shape[-1], v.shape[-1]), jnp.float32)
    _, out = lax.scan(step, init, (to_chunks(q), to_chunks(k), to_chunks(v)))
    return out.transpose(1, 0, 2, 3, 4).reshape(B, S, H, v.shape[-1])

def head_group_norm(y):
    mu = jnp.mean(y, axis=-1, keepdims=True)
    var = jnp.mean(jnp.square(y - mu), axis=-1, keepdims=True)
    return (y - mu) * lax.rsqrt(var + GN_EPS)

def stick_breaking(q, k, v):
    S = q.shape[1]
    scale = q.shape[-1] ** -0.5
    outs = []
    for start in range(0, S, SB_BLOCK):
        end = start + SB_BLOCK
        qb = q[:, start:end]
        kb = k[:, :end]
        vb = v[:, :end]
        z = jnp.einsum('bthd,bshd->bhts', qb, kb) * scale
        t_idx = start + jnp.arange(SB_BLOCK)
        s_idx = jnp.arange(end)
        causal = (s_idx[None, :] < t_idx[:, None])[None, None]
        log_beta = jax.nn.log_sigmoid(z)
        log_1m_beta = jnp.where(causal, log_beta - z, 0.0)
        after = lax.cumsum(log_1m_beta, axis=3, reverse=True) - log_1m_beta
        weights = jnp.where(causal, jnp.exp(log_beta + after), 0.0)
        outs.append(jnp.einsum('bhts,bshe->bthe', weights, vb))
    return jnp.concatenate(outs, axis=1)

def second_inputs(seed: int = 0) -> dict:
    key = jax.random.key(seed)
    ks = jax.random.split(key, 10)
    f32 = jnp.float32
    x = jax.random.normal(ks[0], (BATCH, SEQ, D_MODEL), f32)
    w_in = jax.random.normal(ks[1], (DEPTH, D_MODEL, D_IN_2), f32) * D_MODEL ** -0.5
    p_ret = jax.random.normal(ks[2], (DEPTH, RET_V, D_MODEL), f32) * RET_V ** -0.5
    p_sb = jax.random.normal(ks[3], (DEPTH, SB_W, D_MODEL), f32) * SB_W ** -0.5
    w_out = jax.random.normal(ks[4], (DEPTH, D_MODEL, D_MODEL), f32) * D_MODEL ** -0.5
    w_up = jax.random.normal(ks[5], (DEPTH, D_MODEL, D_FF), f32) * D_MODEL ** -0.5
    w_down = jax.random.normal(ks[6], (DEPTH, D_FF, D_MODEL), f32) * D_FF ** -0.5
    g_mix = 1.0 + 0.02 * jax.random.normal(ks[7], (DEPTH, D_MODEL), f32)
    g_mlp = 1.0 + 0.02 * jax.random.normal(ks[8], (DEPTH, D_MODEL), f32)
    g_final = 1.0 + 0.02 * jax.random.normal(ks[9], (D_MODEL,), f32)
    return {'x': x, 'w_in': w_in, 'p_ret': p_ret, 'p_sb': p_sb, 'w_out': w_out,
            'w_up': w_up, 'w_down': w_down, 'g_mix': g_mix, 'g_mlp': g_mlp,
            'g_final': g_final}

def second_block(x, w_in, p_ret, p_sb, w_out, w_up, w_down, g_mix, g_mlp, g_final):
    B, S, _ = x.shape
    dt = x.dtype
    pos = jnp.arange(S, dtype=jnp.int32)
    log_gamma = jnp.log1p(-(2.0 ** (-5.0 - jnp.arange(RET_HEADS, dtype=jnp.float32))))
    splits = [int(v) for v in np.cumsum(IN_SIZES)[:-1]]
    for l in range(DEPTH):
        h = rmsnorm_2(x, g_mix[l])
        proj = jnp.matmul(h, w_in[l]).astype(jnp.float32)
        q_r, k_r, v_r, g_r, q_s, k_s, v_s, gate_a, gate_b = jnp.split(proj, splits, axis=-1)
        q_r = rotary(q_r.reshape(B, S, RET_HEADS, RET_QK_DIM), pos)
        k_r = rotary(k_r.reshape(B, S, RET_HEADS, RET_QK_DIM), pos) * (RET_QK_DIM ** -0.5)
        ret = retention(q_r, k_r, v_r.reshape(B, S, RET_HEADS, RET_V_DIM), log_gamma)
        ret = head_group_norm(ret).reshape(B, S, RET_V) * jax.nn.silu(g_r)
        sb = stick_breaking(q_s.reshape(B, S, SB_HEADS, SB_HEAD_DIM),
                            k_s.reshape(B, S, SB_HEADS, SB_HEAD_DIM),
                            v_s.reshape(B, S, SB_HEADS, SB_HEAD_DIM)).reshape(B, S, SB_W)
        branch_a = jnp.matmul(ret.astype(dt), p_ret[l]).astype(jnp.float32)
        branch_b = jnp.matmul(sb.astype(dt), p_sb[l]).astype(jnp.float32)
        merged = jax.nn.sigmoid(gate_a) * branch_a + jax.nn.sigmoid(gate_b) * branch_b
        x = x + jnp.matmul(merged.astype(dt), w_out[l]).astype(dt)
        h = rmsnorm_2(x, g_mlp[l])
        up = jnp.square(jax.nn.relu(jnp.matmul(h, w_up[l])))
        x = x + jnp.matmul(up, w_down[l]).astype(dt)
    return rmsnorm_2(x, g_final)


def setup_inputs(seed=0):
    out = dict(first_inputs(seed))
    for name, value in second_inputs(seed + 1).items():
        if name != "x":
            out[name + "_2"] = value
    return out


def reference(
    x, positions, norm_g, w_in, q_norm_g, k_norm_g, lambda_qk, attn_norm_g, w_out_a, conv_w,
    conv_b, igate_b, fgate_b, mlstm_norm_g, w_out_b, w_o, w_in_2, p_ret_2, p_sb_2, w_out_2,
    w_up_2, w_down_2, g_mix_2, g_mlp_2, g_final_2,
):
    x = first_block(
        x, positions, norm_g, w_in, q_norm_g, k_norm_g, lambda_qk, attn_norm_g, w_out_a, conv_w,
        conv_b, igate_b, fgate_b, mlstm_norm_g, w_out_b, w_o,
    )
    return second_block(
        x, w_in_2, p_ret_2, p_sb_2, w_out_2, w_up_2, w_down_2, g_mix_2, g_mlp_2, g_final_2,
    )


_drawn_inputs = setup_inputs


def setup_inputs(seed=0):
    import zlib

    import numpy as np

    out = dict(_drawn_inputs(seed))
    spreads = {}
    factors = {'q_norm_g': 6.205,
     'k_norm_g': 5.398,
     'attn_norm_g': 3.233,
     'conv_b': 5.672,
     'igate_b': 64.0,
     'mlstm_norm_g': 7.953,
     'g_mix_2': 2.984,
     'g_final_2': 7.397,
     'g_mlp_2': 3.921}
    for name, (base, spread) in spreads.items():
        noise = np.random.default_rng([zlib.crc32(name.encode()), seed]).standard_normal(out[name].shape)
        drawn = base * np.exp(spread * noise) if base else spread * noise
        out[name] = __import__('jax').numpy.asarray(drawn.astype(out[name].dtype))
    for name, factor in factors.items():
        out[name] = (out[name] * factor).astype(out[name].dtype)
    return out
```

```python
import math
from contextlib import ExitStack, contextmanager

import numpy as np

import concourse.bass as bass
from concourse import mybir

F32 = mybir.dt.float32
F32R = mybir.dt.float32r
BF16 = mybir.dt.bfloat16
I32 = mybir.dt.int32
ACT = mybir.ActivationFunctionType
ALU = mybir.AluOpType
AX_X = mybir.AxisListType.X

P = 128
D = 1024
S = 512
DEPTH = 2
KT = D // P
TB = S // P
EPS = 1e-6
GN_EPS = 1e-5
BIG_NEG = -1e30

A_HEADS, A_DH, A_DV = 8, 64, 128
B_HEADS, B_DK, B_DV = 8, 64, 128
AQ, AK, AV, AZ, BQK, BV, BI = (D * i for i in range(7))
BO = BI + 2 * B_HEADS
BZ, GA1, GB1 = BO + D, BO + 2 * D, BO + 3 * D
D_IN = GB1 + D
R_HEADS, R_DK, R_DV = 4, 128, 256
S_HEADS, S_DH = 8, 128
QR, KR, VR, GR = 0, 512, 1024, 2048
QS, KS, VS, GA2, GB2 = 3072, 4096, 5120, 6144, 7168
D_IN_2 = 8192
D_FF = 4 * D

QOFF = [0, 128, 384, 768]
SOFF = [0, 512, 1024, 896]
TRI = 1280

RING = 4
A_TAPS = 4

PRM_DMAS = 16
TWO_PI = (6.28125, 0.0019340515136718750, 2 * math.pi - 6.28125 - 0.0019340515136718750)
SIN_MAX = 3.1415925

C_IDENT = 0
C_MQ = 128
C_MS = 256
C_MX = 768
C_GRP = 896
C_TRI = 1024
C_NEG1 = 1152
C_INVF = 1280
C_SGN = 1281
C_EPS = 1282
C_GEPS = 1283
C_ONE = 1284
CST = 1288


def constant_arrays():
    c = np.zeros((P, CST), np.float32)
    i = np.arange(P)
    c[:, C_IDENT:C_IDENT + P] = np.eye(P)
    c[:, C_MQ:C_MQ + P] = np.where(i[None, :] <= i[:, None], 0.0, BIG_NEG)
    key_major = np.where(i[:, None] <= i[None, :], 0.0, BIG_NEG)
    c[:, C_MS:C_MS + TB * P] = np.tile(key_major, (1, TB))
    c[:, C_MX:C_MX + P] = np.where(i[:, None] < i[None, :], 0.0, BIG_NEG)
    c[:, C_GRP:C_GRP + P] = (i[:, None] // 64 == i[None, :] // 64)
    c[:, C_TRI:C_TRI + P] = np.where(i[:, None] >= i[None, :], -1.0, 0.0)
    c[:, C_NEG1:C_NEG1 + P] = -1.0
    c[:, C_INVF] = 10000.0 ** (-2.0 * (i % 32) / A_DH)
    c[:, C_SGN] = np.where(i % 64 < 32, -1.0, 1.0)
    c[:, C_EPS] = EPS
    c[:, C_GEPS] = GN_EPS
    c[:, C_ONE] = 1.0
    inv = (10000.0 ** (-np.arange(64, dtype=np.float64) / 64)).astype(np.float32)
    ang = (np.arange(S, dtype=np.float32)[None, :] * inv[i % 64][:, None]).astype(np.float64)
    rot = np.stack([np.cos(ang), np.sin(ang) * np.where(i < 64, -1.0, 1.0)[:, None]], 1)
    gamma = 1.0 - 2.0 ** (-5.0 - np.arange(R_HEADS))
    diff = np.arange(S)[None, :] - i[:, None]
    dec = np.where(diff[None] >= 0, gamma[:, None, None] ** np.maximum(diff, 0)[None], 0.0)
    dec = (dec * R_DK ** -0.5).transpose(1, 0, 2)
    sel = np.zeros((B_HEADS, B_HEADS, P), np.float32)
    for h in range(B_HEADS):
        sel[h, h] = 1.0
    lam = np.array([[0.8 - 0.6 * math.exp(-0.3 * l)] for l in range(DEPTH)], np.float32)
    return {
        "cst": c,
        "rot2": rot.astype(np.float32),
        "decay": np.ascontiguousarray(dec.astype(np.float32)),
        "sel": sel,
        "lam_init": lam,
    }


class Place:

    def __init__(self, eng):
        self.eng, self.terms, self.n = eng, [], {}

    @contextmanager
    def loop(self, turns, **per):
        with self.eng.Fori(0, turns) as reg:
            start = dict(self.n)
            self.terms.append((reg, per))
            yield reg
            self.terms.pop()
        for k in set(self.n) | set(per):
            grew = self.n.get(k, 0) - start.get(k, 0)
            assert grew == per.get(k, 0), f"one turn adds {grew} to {k}, not {per.get(k, 0)}"
            self.n[k] = start.get(k, 0) + turns * per.get(k, 0)

    def add(self, name, k=1):
        self.n[name] = self.n.get(name, 0) + k
        return k

    def at(self, name, more=0, div=1, times=1):
        v = (self.n.get(name, 0) + more) // div * times
        for reg, per in self.terms:
            k = per.get(name, 0)
            assert k % div == 0, (name, k, div)
            if k:
                v = reg * (k // div * times) + v
        return v

    def slot(self, ring):
        return self.n.get("panel", 0) % ring


PANELS_A = A_HEADS * 4
PANELS_B = (B_HEADS // 2) * 8
PANELS_C = KT * 4
PANELS_D = 2 * 4
PANELS_R = R_HEADS * 12
PANELS_UP = 16
PANELS_DOWN = 2 * 8
PANELS_L1 = PANELS_A + PANELS_B + PANELS_C + PANELS_D
PANELS_L2 = PANELS_R + PANELS_C + PANELS_D + 2 * (PANELS_UP + PANELS_DOWN)


PE_MISC_L1 = 50
PE_MISC_L2 = 24
ACT_L1 = 128
ACT_A = 8
ACT_B = 10
ACT_L2 = 134
ACT_R = 19
DVE_L1 = 235
DVE_A = 11
DVE_B = 25
DVE_L2 = 126
DVE_R = 14


class Region:

    def __init__(self, nc, start, end):
        self.nc, self.cursor, self.end = nc, start, end

    def put(self, name, shape, dt=F32):
        size = int(np.prod(shape[1:])) * (2 if dt == BF16 else 4)
        buf = self.nc.alloc_sbuf_tensor_at(name, shape, dt, offset=self.cursor)
        self.cursor += (size + 31) // 32 * 32
        assert self.cursor <= self.end, (name, self.cursor - self.end)
        return buf


class Memory:

    def __init__(self, nc, ctx):
        tile = KT * S * 4
        base = (nc.sbuf_base + 31) // 32 * 32
        o_x = base
        o_h = o_x + tile
        o_a = o_h + 2 * tile
        o_b = o_a + 2 * tile
        o_w = o_b + 2 * tile
        o_u = o_w + 3 * RING * KT * P * 4
        o_rest = o_u + 2 * tile

        kts, kw = [P, KT, S], [P, RING, KT * P]
        place = Region(nc, o_x, o_h)
        self.x = place.put("x", [P, TB, D])
        place = Region(nc, o_h, o_a)
        self.h_hi = place.put("h_hi", kts, F32R)
        self.h_lo = place.put("h_lo", kts, F32R)
        place = Region(nc, o_a, o_b)
        self.a_hi = place.put("a_hi", kts, F32R)
        self.a_lo = place.put("a_lo", kts, F32R)
        place = Region(nc, o_b, o_w)
        self.b_hi = place.put("b_hi", kts, F32R)
        self.b_lo = place.put("b_lo", kts, F32R)
        place = Region(nc, o_w, o_u)
        self.raw = place.put("raw", kw)
        self.w_hi = place.put("w_hi", kw, F32R)
        self.w_lo = place.put("w_lo", kw, F32R)
        place = Region(nc, o_u, o_rest)
        self.u_hi = place.put("u_hi", kts, F32R)
        self.u_lo = place.put("u_lo", kts, F32R)
        place = Region(nc, o_rest, nc.sbuf_top)
        self.ident = place.put("ident", [P, P])
        self.grp = place.put("grp", [P, P])
        self.ntri = place.put("ntri", [P, P])
        self.neg1 = place.put("neg1", [P, P])
        self.col = place.put("col", [P, 8])
        self.ident_b = place.put("ident_b", [P, P], BF16)
        self.mq_b = place.put("mq_b", [P, P], BF16)
        self.mx_b = place.put("mx_b", [P, P], BF16)
        self.ms_b = place.put("ms_b", [P, TB * P], BF16)
        self.g_norm = place.put("g_norm", [P, KT])
        self.prm = place.put("prm", [P, 8])
        self.conv_w = place.put("conv_w", [P, A_TAPS, KT])
        self.conv_b = place.put("conv_b", [P, KT])
        self.sm = place.put("sm", [P, 96])
        self.gcol = place.put("gcol", [P, B_HEADS, TB])
        self.ecol = place.put("ecol", [P, B_HEADS, TB])
        self.pcol = place.put("pcol", [P, 2, TB])
        end = place.cursor
        place = Region(nc, end, nc.sbuf_top)
        self.cos = place.put("cos", [P, S])
        self.sin = place.put("sin", [P, S])
        at_cos = place.cursor
        place = Region(nc, at_cos, nc.sbuf_top)
        self.negg = place.put("negg", [8, S])
        self.selp = place.put("selp", [8, 2, P])
        place = Region(nc, at_cos, nc.sbuf_top)
        self.sig_a = place.put("sig_a", [P, S])
        self.sig_b = place.put("sig_b", [P, S])
        place = Region(nc, at_cos, nc.sbuf_top)
        self.sp = place.put("sp", [P, TRI])
        place = Region(nc, o_u, o_rest)
        self.xn = place.put("xn", [P, TB, D])
        self.junk = place.put("junk", [P, D])
        place = Region(nc, o_a, o_b)
        self.cst = place.put("cst", [P, CST])
        self.posi = place.put("posi", [P, S], I32)
        self.ang = place.put("ang", [P, S])
        self.turns = place.put("turns", [P, S])
        self.turni = place.put("turni", [P, S], I32)
        self.red = place.put("red", [P, S])
        self.red2 = place.put("red2", [P, S])
        place = Region(nc, o_b, o_w)
        self.wif = place.put("wif", [P, KT, 16])
        self.wif_hi = place.put("wif_hi", [P, KT, 16], F32R)
        self.wif_lo = place.put("wif_lo", [P, KT, 16], F32R)
        self.lqk = place.put("lqk", [P, 4, A_DH])
        self.lqp = place.put("lqp", [P, 2, A_DH])
        self.g16 = place.put("g16", [16, S])
        self.frow = place.put("frow", [8, S])
        self.lrow = place.put("lrow", [8, S])
        self.fcum = place.put("fcum", [8, S])
        self.grow = place.put("grow", [8, S])
        self.erow = place.put("erow", [8, S])
        self.zrow = place.put("zrow", [8, S])
        self.p0 = place.put("p0", [P, TRI])
        self.p1 = place.put("p1", [P, TRI])
        place = Region(nc, o_u, o_rest)
        self.xq = place.put("xq", [P, S])
        self.xk = place.put("xk", [P, S])
        self.sq_q = place.put("sq_q", [P, S])
        self.sq_k = place.put("sq_k", [P, S])
        self.rot_q = place.put("rot_q", [P, S])
        self.rot_k = place.put("rot_k", [P, S])
        self.vT = place.put("vT", [P, S])
        self.v = place.put("v", [P, TB, A_DV])
        self.sg = place.put("sg", [P, S])
        self.sz = place.put("sz", [P, S])
        self.o_sb = place.put("o_sb", [P, TB, A_DV])
        self.o_sq = place.put("o_sq", [P, TB, A_DV])
        place = Region(nc, o_u, o_rest)
        self.yq = place.put("yq", [P, S])
        self.yk = place.put("yk", [P, S])
        self.sgq = place.put("sgq", [P, S])
        self.sgk = place.put("sgk", [P, S])
        self.vTb = place.put("vTb", [P, S])
        self.va0 = place.put("va0", [P, TB, B_DV + 4])
        self.va1 = place.put("va1", [P, TB, B_DV + 4])
        self.e = place.put("e", [P, TRI])
        self.hs = place.put("hs", [P, TB, B_DV])
        self.h_sq = place.put("h_sq", [P, TB, B_DV])
        self.og = place.put("og", [P, S])
        self.zg = place.put("zg", [P, S])
        self.gate = place.put("gate", [P, S])
        place = Region(nc, o_u, o_rest)
        self.stq = place.put("stq", [P, S])
        self.stk = place.put("stk", [P, S])
        self.svT = place.put("svT", [P, S])
        self.sv = place.put("sv", [P, TB, S_DH])
        self.rq = place.put("rq", [P, S])
        self.rk = place.put("rk", [P, S])
        self.rrq = place.put("rrq", [P, S])
        self.rrk = place.put("rrk", [P, S])
        self.rvT0 = place.put("rvT0", [P, S])
        self.rvT1 = place.put("rvT1", [P, S])
        self.rv = place.put("rv", [P, TB, R_DV])
        self.dec = place.put("dec", [P, S])
        self.rg0 = place.put("rg0", [P, S])
        self.rg1 = place.put("rg1", [P, S])
        place = Region(nc, o_u + 4 * S * 4, o_rest)
        self.ro = place.put("ro", [P, TB, R_DV])
        place = Region(nc, o_a, o_w)
        self.up_hi = place.put("up_hi", [P, 16, S], F32R)
        self.up_lo = place.put("up_lo", [P, 16, S], F32R)
        place = Region(nc, o_u, o_rest)
        self.m0 = place.put("m0", [P, S])
        self.m1 = place.put("m1", [P, S])
        self.mm0 = place.put("mm0", [P, S])
        self.mm1 = place.put("mm1", [P, S])
        place = Region(nc, o_a, o_b)
        self.g_fin = place.put("g_fin", [P, D])
        self.va = [self.va0, self.va1]
        self.rvT, self.rg = [self.rvT0, self.rvT1], [self.rg0, self.rg1]
        self.m, self.mm = [self.m0, self.m1], [self.mm0, self.mm1]
        self.bank = [ctx.enter_context(nc.psum_tensor(f"bank{i}", [P, 512], F32)) for i in range(8)]


SEMAPHORES = """
raw_in0 raw_in1 raw_in2 raw_in3 acc_free0 acc_free1 split x_in out_ready out_done used w_step pv_done h_ready
xb_free misc_free xn_ready xT_done sq_ready ss_done vT_ready vT_done qk_ready o_ready scores_done a_ready
p_ready turned v_ready aT_ready on_ready oT_done wif_ready gates_done rows_ready erow_ready pe_step rowsT_done
sel_in hs_ready gb_done bqk_ready bs_done bvT_ready bvT_done bw_ready bv_ready bpv_done bon_ready boT_done
sk_ready z_done svT_ready svT_done sp_ready c_done sw_ready sv_ready so_free so_done rvT_ready rvT_done
rqk_ready rs_done rw_ready rv_ready rpv_done ro_ready roT_done branch_a branch_b u_ready const_in masks_ready
up_ready act_step x_done gain_in rms_ready h_hi_ready prm_in rstd_ready max_ready o_rstd_ready f_in
row_ln_ready rows_m_ready bsig_ready pcol_ready e_ready b_rstd_ready gate_ready og_ready ln_ready sA_ready
sB_ready mask_in pos_in angles_ready sin_ready lam_sum lam_exp rot_q_in rot_k_in sig_ready yq_ready yk_ready
zg_ready table_in dec_in sq_out rotq2_in rotk2_in rsig_ready var_ready r_rstd_ready up_sq_ready gfin_in
dve_step stats_step
""".split()


def program(nc, t, out):
    ctx = ExitStack()
    with ctx:
        m = Memory(nc, ctx)
        s = {name: ctx.enter_context(nc.semaphore(name)) for name in SEMAPHORES}
        raw_in = [s[f"raw_in{i}"] for i in range(RING)]
        acc_free = [s["acc_free0"], s["acc_free1"]]
        acc = [m.bank[0], m.bank[1]]
        misc = m.bank[7]
        st = [m.bank[2][:, 0:512], m.bank[3][:, 0:384], m.bank[4][:, 0:256], m.bank[3][:, 384:512]]
        mst = [m.bank[4][:, 0:512], m.bank[5][:, 0:384], m.bank[6][:, 0:256], m.bank[5][:, 384:512]]
        sq = [[m.bank[4 + k][:, 384:512], m.bank[6][:, 256 * k:256 * k + 256], m.bank[4 + k][:, 0:384],
               m.bank[2 + k][:, 0:512]] for k in range(2)]
        turn = [m.bank[5][:, 384:512], m.bank[6][:, 0:256], m.bank[4][:, 0:384], m.bank[2][:, 0:512]]
        pv = m.bank[3]
        xb = [m.bank[2 + i] for i in range(TB)]
        block = ctx.enter_context(nc.Block())

        w_in = t["w_in"].rearrange("l (k p) n -> l p k n", p=P)
        w_in2 = t["w_in_2"].rearrange("l (k p) n -> l p k n", p=P)
        cols = {name: t[name].rearrange("l (k p) n -> l p k n", p=P)
                for name in ("w_out_a", "w_out_b", "w_o", "p_ret_2", "p_sb_2", "w_out_2", "w_up_2", "w_down_2")}

        @block.sync
        def _(sp):
            at = Place(sp)

            def panel(src):
                slot = at.slot(RING)
                sp.wait_ge(s["split"], at.at("panel", 1))
                sp.dma_start(m.raw[:, slot].rearrange("p (k n) -> p k n", n=src.shape[-1]),
                             src).then_inc(raw_in[slot], 16)
                at.add("panel")

            def column(w, l, col):
                panel(w[bass.ds(l, 1), :, :, bass.ds(col, P)].squeeze(0))

            def rows(w, l, k, col):
                panel(w[bass.ds(l, 1), :, bass.ds(k, 2), bass.ds(col, 512)].squeeze(0))

            def merge(l, gates, ga, gb, wa, wb):
                with at.loop(KT, panel=4) as n:
                    column(gates, l, n * P + ga)
                    column(wa, l, n * P)
                    column(gates, l, n * P + gb)
                    column(wb, l, n * P)

            def project(l, w):
                with at.loop(2, panel=4) as c:
                    for k in range(0, KT, 2):
                        rows(w, l, k, c * 512)

            sp.dma_start(m.x[:], t["x"].rearrange("b (t p) d -> p (b t) d", p=P)).then_inc(s["x_in"], 16)
            with at.loop(DEPTH, panel=PANELS_L1) as l:
                column(w_in, l, AQ)
                column(w_in, l, AK)
                column(w_in, l, AV)
                with at.loop(A_HEADS - 1, panel=4) as i:
                    column(w_in, l, i * P + (AQ + P))
                    column(w_in, l, i * P + (AK + P))
                    column(w_in, l, i * P + (AV + P))
                    column(w_in, l, i * P + AZ)
                column(w_in, l, AZ + (A_HEADS - 1) * P)
                with at.loop(B_HEADS // 2, panel=8) as j:
                    column(w_in, l, j * P + BQK)
                    column(w_in, l, j * P + (BQK + 512))
                    column(w_in, l, j * (2 * P) + BV)
                    column(w_in, l, j * (2 * P) + (BV + P))
                    for a in range(2):
                        column(w_in, l, j * (2 * P) + (BO + a * P))
                        column(w_in, l, j * (2 * P) + (BZ + a * P))
                merge(l, w_in, GA1, GB1, cols["w_out_a"], cols["w_out_b"])
                project(l, cols["w_o"])
            with at.loop(DEPTH, panel=PANELS_L2) as l:
                with at.loop(R_HEADS, panel=12) as i:
                    for a in range(2):
                        column(w_in2, l, i * (2 * P) + (QS + a * P))
                        column(w_in2, l, i * (2 * P) + (KS + a * P))
                        column(w_in2, l, i * (2 * P) + (VS + a * P))
                    column(w_in2, l, i * P + QR)
                    column(w_in2, l, i * P + KR)
                    column(w_in2, l, i * R_DV + VR)
                    column(w_in2, l, i * R_DV + (VR + P))
                    column(w_in2, l, i * R_DV + GR)
                    column(w_in2, l, i * R_DV + (GR + P))
                merge(l, w_in2, GA2, GB2, cols["p_ret_2"], cols["p_sb_2"])
                project(l, cols["w_out_2"])
                with at.loop(2, panel=PANELS_UP + PANELS_DOWN) as f:
                    with at.loop(4, panel=4) as n:
                        for j in range(4):
                            column(cols["w_up_2"], l, f * (16 * P) + n * (4 * P) + j * P)
                    with at.loop(2, panel=8) as c:
                        for k in range(0, 16, 2):
                            rows(cols["w_down_2"], l, f * 16 + k, c * 512)
            for b in range(TB):
                sp.wait_ge(s["out_ready"], b + 1)
                sp.dma_start(out.rearrange("b (t p) d -> p (b t) d", p=P)[:, b], m.xn[:, b]).then_inc(s["out_done"], 16)
            sp.wait_ge(s["out_done"], 16 * TB)
            for i in range(RING):
                sp.wait_ge(raw_in[i], at.at("panel", div=RING, times=16))

        @block.gpsimd
        def _(pool):
            at = Place(pool)
            pool.sem_inc(s["split"], RING)

            def split_panel():
                slot = at.slot(RING)
                pool.wait_ge(s["used"], at.at("panel", 1))
                pool.wait_ge(raw_in[slot], at.at("panel", RING, div=RING, times=16))
                pool.sem_inc(s["w_step"], 1)
                nc.gpsimd.tensor_scalar(m.w_hi[:, slot], m.raw[:, slot], 1.0, 0.0, ALU.mult,
                                        ALU.add).then_inc(s["w_step"], 1)
                pool.wait_ge(s["w_step"], at.at("panel", 1, times=2))
                nc.gpsimd.tensor_tensor(m.w_lo[:, slot], m.raw[:, slot], m.w_hi[:, slot].bitcast(F32),
                                        ALU.subtract).then_inc(s["split"], 1)
                at.add("panel")

            with at.loop((DEPTH * (PANELS_L1 + PANELS_L2)) // RING, panel=RING):
                for _ in range(RING):
                    split_panel()

        @block.tensor
        def _(pe):
            at = Place(pe)
            pe.sem_inc(s["used"], RING)
            pe.sem_inc(s["pv_done"], 1)

            def product(dst, hi, lo, rhs_hi, rhs_lo, first, last):
                nc.tensor.matmul(dst, hi, rhs_lo, start=first, stop=False)
                nc.tensor.matmul(dst, lo, rhs_hi, start=False, stop=False)
                return nc.tensor.matmul(dst, hi, rhs_hi, start=False, stop=last)

            def gemm(x_hi, x_lo, fresh=False):
                slot = at.slot(RING)
                c = at.n.get("acc", 0) % 2
                pe.wait_ge(s["split"], at.at("panel", RING + 1))
                pe.wait_ge(acc_free[c], at.at("acc", 2, div=2))
                for k in range(KT):
                    if fresh:
                        pe.wait_ge(s["h_ready"], at.at("norm", times=KT) + (k + 1))
                    w = slice(k * P, k * P + P)
                    mm = product(acc[c][:], m.w_hi[:, slot, w], m.w_lo[:, slot, w], x_hi[:, k], x_lo[:, k],
                                 k == 0, k == KT - 1)
                mm.then_inc(s["used"], 1)
                at.add("panel")
                at.add("acc")

            def project(x_hi, x_lo, tiles):
                pe.wait_ge(s["xb_free"], at.at("xb", 1))
                for q in range(tiles // 2):
                    slot = at.slot(RING)
                    pe.wait_ge(s["split"], at.at("panel", RING + 1))
                    for k in range(2):
                        w = slice(k * 512, k * 512 + 512)
                        for b in range(TB):
                            kt = 2 * q + k
                            tok = slice(b * P, b * P + P)
                            mm = product(xb[b][:], x_hi[:, kt, tok], x_lo[:, kt, tok], m.w_hi[:, slot, w],
                                         m.w_lo[:, slot, w], kt == 0, kt == tiles - 1)
                    mm.then_inc(s["used"], 1)
                    at.add("panel")
                at.add("xb")

            def misc_bank():
                pe.wait_ge(s["misc_free"], at.at("misc", 1))
                at.add("misc")

            def norm_turns():
                for k in range(KT):
                    if k == 0:
                        pe.wait_ge(s["xn_ready"], at.at("norm", 1))
                    if k >= TB:
                        pe.wait_ge(s["h_ready"], at.at("norm", times=KT) + (k - TB + 1))
                    for b in range(TB):
                        mm = nc.tensor.transpose(xb[k % TB][:, b * P:b * P + P], m.xn[:, b, k * P:k * P + P],
                                                 m.ident[:])
                    mm.then_inc(s["xT_done"], 1)

            def turn4(dst, src):
                for b in range(TB):
                    mm = nc.tensor.transpose(dst[:, b * P:b * P + P], src(b), m.ident[:])
                return mm

            def group_sum(which, sq_buf, ahead):
                pe.wait_ge(s["sq_ready"], at.at("a", ahead, times=2) + (which + 1))
                misc_bank()
                nc.tensor.matmul(misc[:], m.grp[:], sq_buf[:], start=True, stop=True).then_inc(s["ss_done"], 1)

            def value_turns(ahead):
                pe.wait_ge(s["vT_ready"], at.at("a", ahead + 1))
                misc_bank()
                turn4(misc, lambda b: m.vT[:, b * P:b * P + P]).then_inc(s["vT_done"], 1)

            def scores():
                pe.wait_ge(s["qk_ready"], at.at("a", 1))
                pe.wait_ge(s["o_ready"], at.at("a", 1))
                for k in range(2):
                    if k == 1:
                        pe.wait_ge(s["scores_done"], at.at("a", times=2) + 1)
                    r = slice(64 * k, 64 * k + 64)
                    for qb in (3, 2, 1, 0):
                        nc.tensor.matmul(sq[k][qb], m.xq[r, qb * P:qb * P + P], m.xk[r, 0:(qb + 1) * P],
                                         start=True, stop=False)
                        mm = nc.tensor.matmul(sq[k][qb][:, qb * P:qb * P + P], m.ident_b[:], m.mq_b[:],
                                              start=False, stop=True)
                    mm.then_inc(s["scores_done"], 1)

            def weight_turns(qb):
                pe.wait_ge(s["a_ready"], at.at("a", times=4) + (qb + 1))
                if qb == 0:
                    pe.wait_ge(s["p_ready"], at.at("a", times=4) + 3)
                for sb in range(qb + 1):
                    o = QOFF[qb] + sb * P
                    mm = nc.tensor.transpose(turn[qb][:, sb * P:sb * P + P], m.p0[:, o:o + P], m.ident[:])
                mm.then_inc(s["turned"], 1)

            def values(qb):
                if qb == 0:
                    pe.wait_ge(s["v_ready"], at.at("a", 1))
                    pe.wait_ge(s["p_ready"], at.at("a", times=4) + 4)
                pe.wait_ge(s["aT_ready"], at.at("a", times=4) + (qb + 1))
                for sb in range(qb + 1):
                    o = QOFF[qb] + sb * P
                    mm = nc.tensor.matmul(pv[:, qb * P:qb * P + P], m.p1[:, o:o + P], m.v[:, sb],
                                          start=sb == 0, stop=sb == qb)
                if qb == TB - 1:
                    mm.then_inc(s["pv_done"], 1)

            def output_turns():
                pe.wait_ge(s["on_ready"], at.at("a", 1))
                misc_bank()
                turn4(misc, lambda b: m.o_sb[:, b]).then_inc(s["oT_done"], 1)

            def h_gemm():
                gemm(m.h_hi, m.h_lo)

            def gate_rows():
                pe.wait_ge(s["wif_ready"], at.at("layer", 1))
                misc_bank()
                for k in range(KT):
                    mm = product(misc[0:16, :], m.wif_hi[:, k], m.wif_lo[:, k], m.h_hi[:, k], m.h_lo[:, k],
                                 k == 0, k == KT - 1)
                mm.then_inc(s["gates_done"], 1)

            def row_turns():
                pe.wait_ge(s["rows_ready"], at.at("layer", 1))
                pe.wait_ge(s["erow_ready"], at.at("layer", 1))
                misc_bank()
                pe.sem_inc(s["pe_step"], 1)
                for i, row in enumerate((m.grow, m.erow)):
                    for b in range(TB):
                        mm = nc.tensor.transpose(misc[:, (i * TB + b) * 8:(i * TB + b) * 8 + 8],
                                                 row[:, b * P:b * P + P], m.ident[0:8, 0:8])
                mm.then_inc(s["rowsT_done"], 1)

            def spread_gate(a):
                pe.wait_ge(s["sel_in"], at.at("pair", 1, times=16))
                pe.wait_ge(s["hs_ready"], at.at("pair", times=2) + (a + 1))
                nc.tensor.matmul(m.bank[2][:], m.selp[:, a], m.negg[:], start=True, stop=True)
                nc.tensor.matmul(m.bank[3][:], m.selp[:, a], m.negg[:], start=True, stop=False)
                nc.tensor.matmul(m.bank[3][:], m.ident_b[:], m.ms_b[:], start=False,
                                 stop=True).then_inc(s["gb_done"], 1)

            def m_scores(a):
                if a == 0:
                    pe.wait_ge(s["bqk_ready"], at.at("pair", 1))
                r = slice(64 * a, 64 * a + 64)
                for sb in range(TB):
                    mm = nc.tensor.matmul(mst[sb], m.yk[r, sb * P:sb * P + P], m.yq[r, sb * P:S],
                                          start=True, stop=True)
                mm.then_inc(s["bs_done"], 1)

            def m_value_turns(a):
                pe.wait_ge(s["bvT_ready"], at.at("pair", times=2) + (a + 1))
                misc_bank()
                turn4(misc, lambda b: m.vTb[:, b * P:b * P + P]).then_inc(s["bvT_done"], 1)

            def m_values(a):
                pe.wait_ge(s["bw_ready"], at.at("pair", times=2) + (a + 1))
                pe.wait_ge(s["bv_ready"], at.at("pair", times=2) + (a + 1))
                for qb in range(TB):
                    o = (qb % 2) * (B_DV + 4)
                    for sb in range(qb + 1):
                        w = SOFF[sb] + (qb - sb) * P
                        mm = nc.tensor.matmul(m.bank[2 + qb // 2][:, o:o + B_DV + 1], m.e[:, w:w + P],
                                              m.va[a][:, sb, 0:B_DV + 1], start=sb == 0, stop=sb == qb)
                mm.then_inc(s["bpv_done"], 1)

            def m_output_turns(a):
                pe.wait_ge(s["bon_ready"], at.at("pair", times=2) + (a + 1))
                misc_bank()
                turn4(misc, lambda b: m.hs[:, b]).then_inc(s["boT_done"], 1)

            def z_scores(a):
                pe.wait_ge(s["sk_ready"], at.at("r", times=2) + (a + 1))
                for sb in range(TB):
                    nc.tensor.matmul(st[sb], m.stk[:, sb * P:sb * P + P], m.stq[:, sb * P:S],
                                     start=sb < TB - 1, stop=False, skip_group_check=True)
                    mm = nc.tensor.matmul(st[sb][:, 0:P], m.ident_b[:], m.mx_b[:], start=False, stop=True,
                                          skip_group_check=True)
                mm.then_inc(s["z_done"], 1)

            def s_value_turns(a):
                pe.wait_ge(s["svT_ready"], at.at("r", times=2) + (a + 1))
                misc_bank()
                turn4(misc, lambda b: m.svT[:, b * P:b * P + P]).then_inc(s["svT_done"], 1)

            def stick_sums(a):
                pe.wait_ge(s["sp_ready"], at.at("r", times=2) + (a + 1))
                for sb in range(TB):
                    n = S - sb * P
                    mm = nc.tensor.matmul(st[sb], m.ntri[:], m.sp[:, SOFF[sb]:SOFF[sb] + n],
                                          start=False, stop=True, skip_group_check=True)
                    for later in range(sb + 1, TB):
                        n = S - later * P
                        mm = nc.tensor.matmul(st[sb][:, (later - sb) * P:], m.neg1[:],
                                              m.sp[:, SOFF[later]:SOFF[later] + n],
                                              start=False, stop=True, skip_group_check=True)
                mm.then_inc(s["c_done"], 1)

            def s_values(a):
                pe.wait_ge(s["sw_ready"], at.at("r", times=2) + (a + 1))
                pe.wait_ge(s["sv_ready"], at.at("r", times=2) + (a + 1))
                pe.wait_ge(s["so_free"], at.at("r", times=2) + (a + 1))
                for sb in range(TB):
                    n = S - sb * P
                    mm = nc.tensor.matmul(m.bank[5][:, sb * P:S], m.sv[:, sb], m.sp[:, SOFF[sb]:SOFF[sb] + n],
                                          start=sb == 0, stop=sb == TB - 1)
                mm.then_inc(s["so_done"], 1)

            def r_value_turns(half):
                pe.wait_ge(s["rvT_ready"], at.at("r", times=2) + (half + 1))
                misc_bank()
                turn4(misc, lambda b: m.rvT[half][:, b * P:b * P + P]).then_inc(s["rvT_done"], 1)

            def r_scores():
                pe.wait_ge(s["rqk_ready"], at.at("r", 1))
                for sb in range(TB):
                    mm = nc.tensor.matmul(st[sb], m.rk[:, sb * P:sb * P + P], m.rq[:, sb * P:S],
                                          start=True, stop=True)
                mm.then_inc(s["rs_done"], 1)

            def r_values():
                pe.wait_ge(s["rw_ready"], at.at("r", 2))
                pe.wait_ge(s["rv_ready"], at.at("r", 1, times=2))
                for qb in range(TB):
                    o = (qb % 2) * R_DV
                    for sb in range(qb + 1):
                        w = SOFF[sb] + (qb - sb) * P
                        mm = nc.tensor.matmul(m.bank[5 + qb // 2][:, o:o + R_DV], m.sp[:, w:w + P], m.rv[:, sb],
                                              start=sb == 0, stop=sb == qb)
                mm.then_inc(s["rpv_done"], 1)

            def r_output_turns(half):
                if half == 0:
                    pe.wait_ge(s["ro_ready"], at.at("r", 1))
                misc_bank()
                turn4(misc, lambda b: m.ro[:, b, half * P:half * P + P]).then_inc(s["roT_done"], 1)

            def merge():
                with at.loop(KT, panel=4, acc=4):
                    h_gemm()
                    pe.wait_ge(s["branch_a"], at.at("merge", 1, times=KT))
                    gemm(m.a_hi, m.a_lo)
                    h_gemm()
                    pe.wait_ge(s["branch_b"], at.at("merge", 1, times=KT))
                    gemm(m.b_hi, m.b_lo)
                at.add("merge")

            def project_merged():
                with at.loop(2, panel=4, xb=1):
                    pe.wait_ge(s["u_ready"], at.at("merge", times=KT) + 1)
                    project(m.u_hi, m.u_lo, KT)

            def norm():
                norm_turns()

            pe.wait_ge(s["const_in"], 16 * 5)
            pe.wait_ge(s["masks_ready"], 4)
            with at.loop(DEPTH, panel=PANELS_L1, acc=PANELS_L1 - PANELS_D, xb=2, norm=1, layer=1, merge=1,
                         a=A_HEADS, pair=B_HEADS // 2, misc=PE_MISC_L1):
                norm()
                gemm(m.h_hi, m.h_lo, fresh=True)
                at.add("norm")
                h_gemm()
                group_sum(0, m.sq_q, 0)
                h_gemm()
                group_sum(1, m.sq_k, 0)
                value_turns(0)
                gate_rows()
                with at.loop(A_HEADS - 1, panel=4, acc=4, a=1, misc=4):
                    scores()
                    h_gemm()
                    weight_turns(0)
                    weight_turns(1)
                    h_gemm()
                    group_sum(0, m.sq_q, 1)
                    values(0)
                    values(1)
                    weight_turns(2)
                    weight_turns(3)
                    h_gemm()
                    group_sum(1, m.sq_k, 1)
                    values(2)
                    values(3)
                    h_gemm()
                    value_turns(1)
                    output_turns()
                    at.add("a")
                scores()
                h_gemm()
                for qb in range(TB):
                    weight_turns(qb)
                for qb in range(TB):
                    values(qb)
                output_turns()
                at.add("a")

                row_turns()
                at.add("layer")
                with at.loop(B_HEADS // 2, panel=8, acc=8, pair=1, misc=4):
                    h_gemm()
                    h_gemm()
                    h_gemm()
                    spread_gate(0)
                    h_gemm()
                    m_value_turns(0)
                    h_gemm()
                    m_scores(0)
                    m_value_turns(1)
                    h_gemm()
                    m_values(0)
                    spread_gate(1)
                    m_scores(1)
                    h_gemm()
                    m_output_turns(0)
                    m_values(1)
                    h_gemm()
                    m_output_turns(1)
                    at.add("pair")
                merge()
                project_merged()
            with at.loop(DEPTH, panel=PANELS_L2, acc=PANELS_L2 - PANELS_D - 2 * PANELS_DOWN, xb=6, norm=2,
                         merge=1, r=R_HEADS, half=2, misc=PE_MISC_L2):
                norm()
                at.add("norm")
                with at.loop(R_HEADS, panel=12, acc=12, r=1, misc=6):
                    pe.wait_ge(s["h_ready"], at.at("norm", times=KT))
                    h_gemm()
                    h_gemm()
                    h_gemm()
                    z_scores(0)
                    h_gemm()
                    s_value_turns(0)
                    h_gemm()
                    stick_sums(0)
                    h_gemm()
                    s_values(0)
                    z_scores(1)
                    h_gemm()
                    s_value_turns(1)
                    h_gemm()
                    stick_sums(1)
                    h_gemm()
                    s_values(1)
                    h_gemm()
                    r_value_turns(0)
                    r_value_turns(1)
                    r_scores()
                    h_gemm()
                    r_values()
                    h_gemm()
                    r_output_turns(0)
                    r_output_turns(1)
                    at.add("r")
                merge()
                project_merged()
                norm()
                at.add("norm")
                with at.loop(2, panel=PANELS_UP + PANELS_DOWN, acc=16, xb=2, half=1):
                    with at.loop(4, panel=4, acc=4):
                        pe.wait_ge(s["h_ready"], at.at("norm", times=KT))
                        for _ in range(4):
                            h_gemm()
                    with at.loop(2, panel=8, xb=1):
                        pe.wait_ge(s["up_ready"], at.at("half", 1, times=16) + 2)
                        project(m.up_hi, m.up_lo, 16)
                    at.add("half")

        @block.scalar
        def _(act):
            at = Place(act)
            activation = nc.scalar.activation

            def own(ins):
                ins.then_inc(s["act_step"], at.add("own"))
                act.wait_ge(s["act_step"], at.at("own"))

            def log_exp_tables():
                act.preload_act_table_set("natural_log_exp_and_others")

            def panel_done():
                act.wait_ge(s["used"], at.at("panel", RING + 1))
                at.add("panel")
                c = at.n.get("acc", 0) % 2
                at.add("acc")
                return c

            def skip_panel(accumulators=1):
                at.add("panel")
                at.add("acc", accumulators)

            def copy_out(dst, ready, scale=1.0):
                c = panel_done()
                own(activation(dst[:], acc[c][:], ACT.Copy, scale=scale))
                act.sem_inc(acc_free[c], 1)
                act.sem_inc(ready, 1)

            def inv_sqrt(dst, src, scale, eps, ready):
                own(activation(dst, src, ACT.Ln, bias=eps, scale=scale))
                activation(dst, dst, ACT.Exp, scale=-0.5).then_inc(ready, 1)

            def norm(gain):
                act.wait_ge(s["x_done"], at.at("proj", 1, times=KT))
                act.dma_start(m.g_norm[:], gain, allow_slow_non_contiguous=True).then_inc(s["gain_in"], 16)
                for b in range(TB):
                    own(activation(m.junk[:], m.x[:, b], ACT.Square, accum_out=m.sm[:, b:b + 1]))
                inv_sqrt(m.sm[:, 4:8], m.sm[:, 0:4], 1.0 / D, m.col[:, 2:3], s["rms_ready"])
                act.wait_ge(s["gain_in"], at.at("norm", 1, times=16))
                for k in range(KT):
                    act.wait_ge(s["xT_done"], at.at("norm", times=KT) + (k + 1))
                    activation(m.h_hi[:, k], xb[k % TB][:], ACT.Copy,
                               scale=m.g_norm[:, k:k + 1]).then_inc(s["h_hi_ready"], 1)
                at.add("norm")

            def column(name, l, n=None):
                a = t[name].rearrange("l (k p) -> l p k", p=n or P)
                return a[bass.ds(l, 1)].squeeze(0)

            def layer_parameters(l):
                def load(dst, src):
                    act.dma_start(dst, src, allow_slow_non_contiguous=True).then_inc(s["prm_in"], 16)

                for i, name in enumerate(("q_norm_g", "k_norm_g")):
                    for half in range(2):
                        load(m.prm[64 * half:64 * half + 64, i:i + 1], column(name, l, A_DH))
                load(m.prm[:, 6:7], column("attn_norm_g", l))
                load(m.prm[:, 3:4], column("mlstm_norm_g", l))
                load(m.prm[0:8, 4:5], column("igate_b", l, 8))
                load(m.prm[8:16, 4:5], column("fgate_b", l, 8))
                load(m.prm[:, 5:6], t["lam_init"][bass.ds(l, 1)].to_broadcast([P, 1]))
                load(m.lqk[:].rearrange("p a b -> p (a b)"),
                     t["lambda_qk"].rearrange("l a b -> l (a b)")[bass.ds(l, 1)].to_broadcast([P, 4 * A_DH]))
                for tap in range(A_TAPS):
                    load(m.conv_w[:, tap], t["conv_w"].rearrange("l j (k p) -> l j p k", p=P)[bass.ds(l, 1), tap].squeeze(0))
                load(m.conv_b[:], column("conv_b", l))
                load(m.wif[:], w_in[bass.ds(l, 1), :, :, BI:BI + 16].squeeze(0))

            def rotate_halves(dst, src, ready, half):
                for g in range(P // half):
                    act.dma_start(dst[half * g:half * g + half], src[half * (g ^ 1):half * (g ^ 1) + half]).then_inc(ready, 16)

            def qk_out(which, dst, sq_buf, rot, ready):
                c = panel_done()
                activation(sq_buf[:], acc[c][:], ACT.Square).then_inc(s["sq_ready"], 1)
                own(activation(dst[:], acc[c][:], ACT.Copy, scale=m.prm[:, which:which + 1]))
                act.sem_inc(acc_free[c], 1)
                rotate_halves(rot, dst, ready, 32)

            def group_rstd(which, sq_buf, ahead):
                act.wait_ge(s["ss_done"], at.at("a", ahead, times=2) + (which + 1))
                own(activation(sq_buf[:], misc[:], ACT.Ln, bias=m.col[:, 2:3], scale=1.0 / A_DH))
                act.sem_inc(s["misc_free"], 1)
                activation(sq_buf[:], sq_buf[:], ACT.Exp, scale=-0.5).then_inc(s["rstd_ready"], 1)

            def values_out(ahead):
                act.wait_ge(s["vT_done"], at.at("a", ahead + 1))
                own(activation(m.v[:].rearrange("p b e -> p (b e)"), misc[:], ACT.Copy))
                act.sem_inc(s["misc_free"], 1)
                act.sem_inc(s["v_ready"], 1)

            def exponentials():
                act.wait_ge(s["max_ready"], at.at("a", 1))
                act.wait_ge(s["pv_done"], at.at("a", 1))
                for qb in range(TB):
                    for k, p in enumerate((m.p0, m.p1)):
                        i = 4 * k + qb
                        ins = activation(p[:, QOFF[qb]:QOFF[qb] + (qb + 1) * P], sq[k][qb], ACT.Exp,
                                         bias=m.sm[:, 20 + i:21 + i], scale=A_DH ** -0.5,
                                         accum_out=m.sm[:, 28 + i:29 + i])
                    ins.then_inc(s["p_ready"], 1)

            def turned_out(qb):
                act.wait_ge(s["turned"], at.at("a", times=4) + (qb + 1))
                activation(m.p1[:, QOFF[qb]:QOFF[qb] + (qb + 1) * P], turn[qb], ACT.Copy).then_inc(s["aT_ready"], 1)

            def head_rstd():
                act.wait_ge(s["o_ready"], at.at("a", 2))
                for b in range(TB):
                    ins = activation(m.o_sq[:, b], m.o_sb[:, b], ACT.Square, accum_out=m.sm[:, 48 + b:49 + b])
                own(ins)
                inv_sqrt(m.sm[:, 52:56], m.sm[:, 48:52], 1.0 / A_DV, m.col[:, 2:3], s["o_rstd_ready"])

            def sigmoid_out(dst, ready, free):
                c = panel_done()
                ins = activation(dst[:], acc[c][:], ACT.Sigmoid)
                if free:
                    own(ins)
                    act.sem_inc(acc_free[c], 1)
                    act.sem_inc(ready, 1)
                else:
                    ins.then_inc(ready, 1)

            def gate_rows():
                act.wait_ge(s["gates_done"], at.at("layer", 1))
                own(activation(m.g16[:], misc[0:16, :], ACT.Identity, bias=m.prm[0:16, 4:5]))
                act.sem_inc(s["misc_free"], 1)
                act.dma_start(m.frow[:], m.g16[8:16]).then_inc(s["f_in"], 16)
                act.wait_ge(s["f_in"], at.at("layer", 1, times=16))
                own(activation(m.lrow[:], m.frow[:], ACT.Abs))
                own(activation(m.lrow[:], m.lrow[:], ACT.Exp, scale=-1.0))
                activation(m.lrow[:], m.lrow[:], ACT.Ln, bias=m.col[0:8, 4:5]).then_inc(s["row_ln_ready"], 1)

            def gate_floor():
                act.wait_ge(s["rows_m_ready"], at.at("layer", 1))
                activation(m.erow[:], m.erow[:], ACT.Exp, scale=-1.0).then_inc(s["erow_ready"], 1)

            def m_sigmoid(src, dst, ready_src):
                act.wait_ge(ready_src, at.at("pair", 1))
                activation(dst[:], src[:], ACT.Sigmoid).then_inc(s["bsig_ready"], 1)

            def m_decays(a):
                act.wait_ge(s["gb_done"], at.at("pair", times=2) + (a + 1))
                act.wait_ge(s["pcol_ready"], at.at("pair", 1))
                for sb in range(TB):
                    bias, o = m.pcol[:, a, sb:sb + 1], SOFF[sb]
                    ins = activation(m.e[:, o:o + P], m.bank[3][:, sb * P:sb * P + P], ACT.Exp, bias=bias)
                    if sb < TB - 1:
                        ins = activation(m.e[:, o + P:o + S - sb * P], m.bank[2][:, (sb + 1) * P:S], ACT.Exp, bias=bias)
                ins.then_inc(s["e_ready"], 1)

            def m_values_out(a):
                act.wait_ge(s["bvT_done"], at.at("pair", times=2) + (a + 1))
                own(activation(m.va[a][:, :, 0:B_DV], misc[:].rearrange("p (b e) -> p b e", e=P), ACT.Copy))
                act.sem_inc(s["misc_free"], 1)
                act.sem_inc(s["bv_ready"], 1)

            def m_rstd(a):
                act.wait_ge(s["hs_ready"], at.at("pair", times=2) + (a + 2))
                for b in range(TB):
                    ins = activation(m.h_sq[:, b], m.hs[:, b], ACT.Square, accum_out=m.sm[:, 68 + b:69 + b])
                own(ins)
                inv_sqrt(m.sm[:, 72:76], m.sm[:, 68:72], 1.0 / B_DV, m.col[:, 2:3], s["b_rstd_ready"])

            def m_o_gate(a):
                act.wait_ge(s["gate_ready"], at.at("pair", times=2) + (a + 1))
                sigmoid_out(m.og, s["og_ready"], free=True)

            def softplus_parts(a):
                act.wait_ge(s["z_done"], at.at("r", times=2) + (a + 1))
                activation(m.sp[:, 0:512], m.bank[2][:], ACT.Abs)
                activation(m.sp[:, 512:1024], m.bank[3][:], ACT.Abs)
                own(activation(m.sp[:, 1024:1280], m.bank[4][:, 0:256], ACT.Abs))
                own(activation(m.sp[:], m.sp[:], ACT.Exp, scale=-1.0))
                activation(m.sp[:], m.sp[:], ACT.Ln, bias=m.col[:, 4:5]).then_inc(s["ln_ready"], 1)

            def stick_weights(a):
                act.wait_ge(s["c_done"], at.at("r", times=2) + (a + 1))
                activation(m.sp[:, 0:512], m.bank[2][:], ACT.Exp)
                activation(m.sp[:, 512:1024], m.bank[3][:], ACT.Exp)
                activation(m.sp[:, 1024:1280], m.bank[4][:, 0:256], ACT.Exp).then_inc(s["sw_ready"], 1)

            def s_values_out(a):
                act.wait_ge(s["svT_done"], at.at("r", times=2) + (a + 1))
                own(activation(m.sv[:].rearrange("p b e -> p (b e)"), misc[:], ACT.Copy))
                act.sem_inc(s["misc_free"], 1)
                act.sem_inc(s["sv_ready"], 1)

            def r_qk_out(dst, rot, ready):
                c = panel_done()
                own(activation(dst[:], acc[c][:], ACT.Copy))
                act.sem_inc(acc_free[c], 1)
                rotate_halves(rot, dst, ready, 64)

            def r_values_out(half):
                act.wait_ge(s["rvT_done"], at.at("r", times=2) + (half + 1))
                own(activation(m.rv[:, :, half * P:half * P + P], misc[:].rearrange("p (b e) -> p b e", e=P), ACT.Copy))
                act.sem_inc(s["misc_free"], 1)
                act.sem_inc(s["rv_ready"], 1)

            def merge():
                with at.loop(KT, panel=4, acc=4, u=1, own=2):
                    act.wait_ge(s["u_ready"], at.at("u", 1))
                    sigmoid_out(m.sig_a, s["sA_ready"], free=True)
                    skip_panel()
                    sigmoid_out(m.sig_b, s["sB_ready"], free=True)
                    skip_panel()
                    at.add("u")
                at.add("panel", PANELS_D)
                at.add("proj")

            cst = t["cst"]
            for dst, c in ((m.ident, C_IDENT), (m.grp, C_GRP), (m.ntri, C_TRI), (m.neg1, C_NEG1)):
                act.dma_start(dst[:], cst[:, c:c + P]).then_inc(s["const_in"], 16)
            act.dma_start(m.col[:], cst[:, C_INVF:C_INVF + 8]).then_inc(s["const_in"], 16)
            act.dma_start(m.cst[:, C_MQ:C_MX + P], cst[:, C_MQ:C_MX + P]).then_inc(s["mask_in"], 16)
            act.dma_start(m.posi[:], t["positions"].to_broadcast([P, S])).then_inc(s["pos_in"], 16)
            act.wait_ge(s["const_in"], 16 * 5)
            act.wait_ge(s["angles_ready"], 2)
            activation(m.sin[:], m.red[:], ACT.Sin)
            activation(m.cos[:], m.red2[:], ACT.Sin).then_inc(s["sin_ready"], 1)

            with at.loop(DEPTH, panel=PANELS_L1, acc=PANELS_L1 - PANELS_D, norm=1, proj=1, layer=1, a=A_HEADS,
                         pair=B_HEADS // 2, u=KT, own=ACT_L1) as l:
                log_exp_tables()
                norm(column("norm_g", l))
                layer_parameters(l)
                act.wait_ge(s["prm_in"], at.at("layer", 1, times=PRM_DMAS * 16))
                act.wait_ge(s["lam_sum"], at.at("layer", 1))
                activation(m.sm[:, 10:12], m.sm[:, 8:10], ACT.Exp).then_inc(s["lam_exp"], 1)
                qk_out(0, m.xq, m.sq_q, m.rot_q, s["rot_q_in"])
                qk_out(1, m.xk, m.sq_k, m.rot_k, s["rot_k_in"])
                group_rstd(0, m.sq_q, 0)
                copy_out(m.vT, s["vT_ready"])
                group_rstd(1, m.sq_k, 0)
                values_out(0)
                gate_rows()
                gate_floor()
                with at.loop(A_HEADS - 1, panel=4, acc=4, a=1, own=ACT_A):
                    log_exp_tables()
                    exponentials()
                    qk_out(0, m.xq, m.sq_q, m.rot_q, s["rot_q_in"])
                    turned_out(0)
                    turned_out(1)
                    qk_out(1, m.xk, m.sq_k, m.rot_k, s["rot_k_in"])
                    group_rstd(0, m.sq_q, 1)
                    turned_out(2)
                    turned_out(3)
                    copy_out(m.vT, s["vT_ready"])
                    group_rstd(1, m.sq_k, 1)
                    head_rstd()
                    sigmoid_out(m.sg, s["sig_ready"], free=False)
                    values_out(1)
                    at.add("a")
                log_exp_tables()
                exponentials()
                for qb in range(TB):
                    turned_out(qb)
                head_rstd()
                sigmoid_out(m.sg, s["sig_ready"], free=False)
                at.add("a")
                at.add("layer")

                with at.loop(B_HEADS // 2, panel=8, acc=8, pair=1, own=ACT_B) as j:
                    act.dma_start(m.selp[:], t["sel"][:, bass.ds(j * 2, 2)]).then_inc(s["sel_in"], 16)
                    skip_panel()
                    m_sigmoid(m.yq, m.sgq, s["yq_ready"])
                    skip_panel()
                    m_sigmoid(m.yk, m.sgk, s["yk_ready"])
                    copy_out(m.vTb, s["bvT_ready"])
                    log_exp_tables()
                    m_decays(0)
                    m_values_out(0)
                    copy_out(m.vTb, s["bvT_ready"])
                    m_o_gate(0)
                    m_values_out(1)
                    sigmoid_out(m.zg, s["zg_ready"], free=False)
                    log_exp_tables()
                    m_decays(1)
                    m_rstd(0)
                    m_o_gate(1)
                    log_exp_tables()
                    m_rstd(1)
                    sigmoid_out(m.zg, s["zg_ready"], free=False)
                    at.add("pair")
                merge()

            act.wait_ge(s["x_done"], KT * (DEPTH + 1))
            act.dma_start(m.cos[:], t["rot2"][:, 0]).then_inc(s["table_in"], 16)
            act.dma_start(m.sin[:], t["rot2"][:, 1]).then_inc(s["table_in"], 16)
            with at.loop(DEPTH, panel=PANELS_L2, acc=PANELS_L2 - PANELS_D - 2 * PANELS_DOWN, norm=2, proj=3,
                         r=R_HEADS, u=KT, up=32, own=ACT_L2) as l:
                log_exp_tables()
                norm(column("g_mix_2", l))
                with at.loop(R_HEADS, panel=12, acc=12, r=1, own=ACT_R) as i:
                    log_exp_tables()
                    act.wait_ge(s["rw_ready"], at.at("r", 1))
                    act.dma_start(m.dec[:], t["decay"][:, bass.ds(i, 1)].squeeze(1)).then_inc(s["dec_in"], 16)
                    copy_out(m.stq, s["sq_out"], scale=S_DH ** -0.5)
                    copy_out(m.stk, s["sk_ready"])
                    copy_out(m.svT, s["svT_ready"])
                    softplus_parts(0)
                    copy_out(m.stq, s["sq_out"], scale=S_DH ** -0.5)
                    s_values_out(0)
                    copy_out(m.stk, s["sk_ready"])
                    stick_weights(0)
                    copy_out(m.svT, s["svT_ready"])
                    softplus_parts(1)
                    r_qk_out(m.rq, m.rrq, s["rotq2_in"])
                    s_values_out(1)
                    r_qk_out(m.rk, m.rrk, s["rotk2_in"])
                    stick_weights(1)
                    copy_out(m.rvT[0], s["rvT_ready"])
                    copy_out(m.rvT[1], s["rvT_ready"])
                    r_values_out(0)
                    r_values_out(1)
                    sigmoid_out(m.rg[0], s["rsig_ready"], free=False)
                    log_exp_tables()
                    act.wait_ge(s["var_ready"], at.at("r", 1))
                    inv_sqrt(m.sm[:, 64:68], m.sm[:, 56:64].rearrange("p (b k) -> p b k", k=2)[:, :, 1], 1.0,
                             m.col[:, 3:4], s["r_rstd_ready"])
                    sigmoid_out(m.rg[1], s["rsig_ready"], free=False)
                    at.add("r")
                merge()
                log_exp_tables()
                norm(column("g_mlp_2", l))
                with at.loop(2, panel=PANELS_UP + PANELS_DOWN, acc=16, up=16, proj=1, own=16):
                    with at.loop(4, panel=4, acc=4, up=4, own=4):
                        for j in range(4):
                            c = panel_done()
                            act.wait_ge(s["up_ready"], at.at("up", 1))
                            own(activation(m.m[j % 2][:], acc[c][:], ACT.Relu))
                            act.sem_inc(acc_free[c], 1)
                            activation(m.mm[j % 2][:], m.m[j % 2][:], ACT.Square).then_inc(s["up_sq_ready"], 1)
                            at.add("up")
                    at.add("panel", PANELS_DOWN)
                    at.add("proj")
            log_exp_tables()
            act.wait_ge(s["x_done"], at.at("proj", 1, times=KT))
            act.dma_start(m.g_fin[:], t["g_final_2"].rearrange("(a d) -> a d", a=1).to_broadcast([P, D])).then_inc(s["gfin_in"], 16)
            for b in range(TB):
                own(activation(m.junk[:], m.x[:, b], ACT.Square, accum_out=m.sm[:, b:b + 1]))
            inv_sqrt(m.sm[:, 4:8], m.sm[:, 0:4], 1.0 / D, m.col[:, 2:3], s["rms_ready"])

        @block.vector
        def _(dve):
            at = Place(dve)
            tt, ts, stt = nc.vector.tensor_tensor, nc.vector.tensor_scalar, nc.vector.scalar_tensor_tensor
            for name, credit in (("acc_free0", 1), ("acc_free1", 1), ("misc_free", 1), ("o_ready", 1), ("hs_ready", 1),
                                 ("xb_free", 1), ("u_ready", 1), ("up_ready", 2), ("rw_ready", 1), ("gate_ready", 1), ("so_free", 1)):
                dve.sem_inc(s[name], credit)

            def own(ins):
                ins.then_inc(s["dve_step"], at.add("own"))
                dve.wait_ge(s["dve_step"], at.at("own"))

            def panel_done():
                dve.wait_ge(s["used"], at.at("panel", RING + 1))
                return take_panel()

            def take_panel():
                at.add("panel")
                c = at.n.get("acc", 0) % 2
                at.add("acc")
                return c

            def split(hi, lo, src, ready):
                own(ts(hi, src, 1.0, None, ALU.mult))
                tt(lo, src, hi.bitcast(F32), ALU.subtract).then_inc(ready, 1)

            def tile(buf, k):
                return buf[:, bass.ds(k, 1)].squeeze(1) if not isinstance(k, int) else buf[:, k]

            def norm():
                dve.wait_ge(s["rms_ready"], at.at("norm", 1))
                for b in range(TB):
                    ins = ts(m.xn[:, b], m.x[:, b], m.sm[:, 4 + b:5 + b], None, ALU.mult)
                ins.then_inc(s["xn_ready"], 1)
                for k in range(KT):
                    dve.wait_ge(s["h_hi_ready"], at.at("norm", times=KT) + (k + 1))
                    stt(m.h_lo[:, k], xb[k % TB][:], m.g_norm[:, k:k + 1], m.h_hi[:, k].bitcast(F32), ALU.mult,
                        ALU.subtract).then_inc(s["h_ready"], 1)
                at.add("norm")

            def add_to_x():
                with at.loop(2, panel=4 if at.tiles == KT else 8, proj4=1, own=1) as c:
                    at.add("panel", at.tiles // 2)
                    dve.wait_ge(s["used"], at.at("panel", RING))
                    for b in range(TB):
                        xs = m.x[:, b, bass.ds(c * 512, 512)]
                        ins = tt(xs, xs, xb[b][:], ALU.add)
                        if b < TB - 1:
                            ins.then_inc(s["x_done"], 1)
                    own(ins)
                    dve.sem_inc(s["x_done"], 1)
                    dve.sem_inc(s["xb_free"], 1)
                    at.add("proj4")

            def lambdas():
                dve.wait_ge(s["prm_in"], at.at("layer", 1, times=PRM_DMAS * 16))
                own(ts(m.wif_hi[:], m.wif[:], 1.0, None, ALU.mult))
                tt(m.wif_lo[:], m.wif[:], m.wif_hi[:].bitcast(F32), ALU.subtract).then_inc(s["wif_ready"], 1)
                own(tt(m.lqp[:], m.lqk[:].rearrange("p (a two) d -> p a two d", two=2)[:, :, 0],
                       m.lqk[:].rearrange("p (a two) d -> p a two d", two=2)[:, :, 1], ALU.mult))
                nc.vector.tensor_reduce(m.sm[:, 8:10], m.lqp[:], AX_X, ALU.add).then_inc(s["lam_sum"], 1)
                own(ts(m.prm[:, 2:3], m.prm[:, 5:6], -1.0, 1.0, ALU.mult, ALU.add))
                own(tt(m.prm[:, 2:3], m.prm[:, 2:3], m.prm[:, 6:7], ALU.mult))
                nc.vector.memset(m.zrow[:], 0.0).then_inc(s["dve_step"], at.add("own"))
                dve.wait_ge(s["lam_exp"], at.at("layer", 1))
                own(tt(m.prm[:, 7:8], m.sm[:, 11:12], m.sm[:, 10:11], ALU.subtract))
                own(tt(m.prm[:, 7:8], m.prm[:, 7:8], m.prm[:, 5:6], ALU.subtract))

            def gate_rows():
                dve.wait_ge(s["row_ln_ready"], at.at("layer", 1))
                own(ts(m.fcum[:], m.frow[:], 0.0, None, ALU.min))
                own(tt(m.fcum[:], m.fcum[:], m.lrow[:], ALU.subtract))
                own(nc.vector.tensor_tensor_scan(m.frow[:], m.fcum[:], m.zrow[:], 0.0, ALU.add, ALU.add))
                own(tt(m.grow[:], m.g16[0:8], m.frow[:], ALU.subtract))
                own(nc.vector.tensor_tensor_scan(m.erow[:], m.grow[:], m.grow[:], BIG_NEG, ALU.max, ALU.max))
                ts(m.negg[:], m.erow[:], -1.0, None, ALU.mult).then_inc(s["rows_ready"], 1)
                tt(m.erow[:], m.erow[:], m.frow[:], ALU.add).then_inc(s["rows_m_ready"], 1)

            def rotate(x, rot, cos, sin, rstd, last):
                tt(x[:], x[:], cos[:], ALU.mult)
                own(tt(rot[:], rot[:], sin[:], ALU.mult))
                ins = tt(x[:], x[:], rot[:], ALU.add)
                if rstd is not None:
                    own(ins)
                    dve.wait_ge(*rstd[1])
                    ins = tt(x[:], x[:], rstd[0][:], ALU.mult)
                if last is None:
                    own(ins)
                else:
                    ins.then_inc(last, 1)

            def rotate_qk(which, ahead):
                x, rot, sqb = ((m.xq, m.rot_q, m.sq_q), (m.xk, m.rot_k, m.sq_k))[which]
                dve.wait_ge(s["rot_k_in" if which else "rot_q_in"], at.at("a", ahead + 1, times=64))
                rotate(x, rot, m.cos, m.sin,
                       (sqb, (s["rstd_ready"], at.at("a", ahead, times=2) + (which + 1))),
                       s["qk_ready"] if which else None)

            def maxima():
                dve.wait_ge(s["scores_done"], at.at("a", times=2) + 1)
                for qb in (3, 2, 0):
                    nc.vector.tensor_reduce(m.sm[:, 12 + qb:13 + qb], sq[0][qb], AX_X, ALU.max)
                dve.wait_ge(s["scores_done"], at.at("a", times=2) + 2)
                nc.vector.tensor_reduce(m.sm[:, 13:14], sq[0][1], AX_X, ALU.max)
                for qb in (3, 2, 1, 0):
                    ins = nc.vector.tensor_reduce(m.sm[:, 16 + qb:17 + qb], sq[1][qb], AX_X, ALU.max)
                own(ins)
                ts(m.sm[:, 20:28], m.sm[:, 12:20], -(A_DH ** -0.5), None, ALU.mult).then_inc(s["max_ready"], 1)

            def combine():
                dve.wait_ge(s["p_ready"], at.at("a", 1, times=4))
                own(nc.vector.reciprocal(m.sm[:, 36:44], m.sm[:, 28:36]))
                own(stt(m.sm[:, 44:48], m.sm[:, 28:32], m.prm[:, 7:8], m.sm[:, 40:44], ALU.mult, ALU.mult))
                for qb in range(TB):
                    w = slice(QOFF[qb], QOFF[qb] + (qb + 1) * P)
                    stt(m.p0[:, w], m.p1[:, w], m.sm[:, 44 + qb:45 + qb], m.p0[:, w], ALU.mult,
                        ALU.add).then_inc(s["a_ready"], 1)

            def head_output():
                dve.wait_ge(s["pv_done"], at.at("a", 2))
                tt(m.o_sb[:], pv[:].rearrange("p (b e) -> p b e", e=P),
                   m.sm[:, 36:40].unsqueeze(2).to_broadcast([P, TB, P]), ALU.mult).then_inc(s["o_ready"], 1)

            def head_normalised():
                dve.wait_ge(s["o_rstd_ready"], at.at("a", 1))
                tt(m.o_sb[:], m.o_sb[:], m.sm[:, 52:56].unsqueeze(2).to_broadcast([P, TB, P]),
                   ALU.mult).then_inc(s["on_ready"], 1)

            def head_gate():
                dve.wait_ge(s["sig_ready"], at.at("a", 1))
                c = take_panel()
                own(tt(m.sz[:], acc[c][:], m.sg[:], ALU.mult))
                dve.sem_inc(acc_free[c], 1)

            def head_branch(k):
                dve.wait_ge(s["oT_done"], at.at("a", 1))
                own(stt(m.sz[:], misc[:], m.prm[:, 2:3], m.sz[:], ALU.mult, ALU.mult))
                dve.sem_inc(s["misc_free"], 1)
                split(tile(m.a_hi, k), tile(m.a_lo, k), m.sz[:], s["branch_a"])

            def convolve(y, kt, ready):
                c = panel_done()
                a = acc[c]
                w = [m.conv_w[:, tap, bass.ds(kt, 1)] for tap in range(A_TAPS)]
                own(ts(y[:], a[:], w[A_TAPS - 1], m.conv_b[:, bass.ds(kt, 1)], ALU.mult, ALU.add))
                for tap in range(A_TAPS - 2, -1, -1):
                    d = A_TAPS - 1 - tap
                    own(stt(y[:, d:], a[:, :S - d], w[tap], y[:, d:], ALU.mult, ALU.add))
                dve.sem_inc(acc_free[c], 1)
                dve.sem_inc(ready, 1)

            def m_weights(a):
                dve.wait_ge(s["e_ready"], at.at("pair", times=2) + (a + 1))
                dve.wait_ge(s["bs_done"], at.at("pair", times=2) + (a + 1))
                for sb in range(TB):
                    w = slice(SOFF[sb], SOFF[sb] + S - sb * P)
                    ins = tt(m.e[:, w], mst[sb], m.e[:, w], ALU.mult)
                ins.then_inc(s["bw_ready"], 1)

            def m_output(j, a):
                dve.wait_ge(s["bpv_done"], at.at("pair", times=2) + (a + 1))
                outs = [m.bank[2 + k][:, 0:2 * (B_DV + 4)].rearrange("p (b e) -> p b e", e=B_DV + 4) for k in range(2)]
                den, mag = m.sm[:, 56:60], m.sm[:, 60:64]
                for k in range(2):
                    ins = nc.vector.tensor_copy(den[:, 2 * k:2 * k + 2], outs[k][:, :, B_DV])
                own(ins)
                own(stt(mag, den, -1.0, den, ALU.mult, ALU.max))
                own(tt(mag, mag, m.ecol[:, bass.ds(j * 2 + a, 1)].squeeze(1), ALU.max))
                own(nc.vector.reciprocal(den, mag))
                for k in range(2):
                    ins = tt(m.hs[:, 2 * k:2 * k + 2], outs[k][:, :, 0:B_DV],
                             den[:, 2 * k:2 * k + 2].unsqueeze(2).to_broadcast([P, 2, B_DV]), ALU.mult)
                ins.then_inc(s["hs_ready"], 1)

            def m_normalised(a):
                dve.wait_ge(s["b_rstd_ready"], at.at("pair", times=2) + (a + 1))
                tt(m.hs[:], m.hs[:], m.sm[:, 72:76].unsqueeze(2).to_broadcast([P, TB, B_DV]),
                   ALU.mult).then_inc(s["bon_ready"], 1)

            def m_gate(a):
                dve.wait_ge(s["zg_ready"], at.at("pair", times=2) + (a + 1))
                take_panel()
                c = take_panel()
                own(tt(m.gate[:], acc[c][:], m.zg[:], ALU.mult))
                dve.sem_inc(acc_free[c], 1)
                dve.wait_ge(s["og_ready"], at.at("pair", times=2) + (a + 1))
                own(tt(m.gate[:], m.gate[:], m.og[:], ALU.mult))
                dve.sem_inc(s["gate_ready"], 1)

            def m_branch(j, a):
                dve.wait_ge(s["boT_done"], at.at("pair", times=2) + (a + 1))
                own(stt(m.gate[:], misc[:], m.prm[:, 3:4], m.gate[:], ALU.mult, ALU.mult))
                dve.sem_inc(s["misc_free"], 1)
                split(tile(m.b_hi, j * 2 + a), tile(m.b_lo, j * 2 + a), m.gate[:], s["branch_b"])

            def merge():
                with at.loop(KT, panel=4, acc=4, u=1, own=4) as n:
                    dve.wait_ge(s["sA_ready"], at.at("u", 1))
                    take_panel()
                    c = panel_done()
                    own(tt(m.sig_a[:], acc[c][:], m.sig_a[:], ALU.mult))
                    dve.sem_inc(acc_free[c], 1)
                    dve.wait_ge(s["sB_ready"], at.at("u", 1))
                    take_panel()
                    c = panel_done()
                    own(tt(m.sig_b[:], acc[c][:], m.sig_b[:], ALU.mult))
                    dve.sem_inc(acc_free[c], 1)
                    own(tt(m.sig_a[:], m.sig_a[:], m.sig_b[:], ALU.add))
                    split(tile(m.u_hi, n), tile(m.u_lo, n), m.sig_a[:], s["u_ready"])
                    at.add("u")

            def softplus(a):
                dve.wait_ge(s["ln_ready"], at.at("r", times=2) + (a + 1))
                for i, n in enumerate((512, 512, 256)):
                    w = slice(512 * i, 512 * i + n)
                    ins = stt(m.sp[:, w], m.bank[2 + i][:, 0:n], 0.0, m.sp[:, w], ALU.max, ALU.add)
                ins.then_inc(s["sp_ready"], 1)

            def stick_branch(i, a):
                dve.wait_ge(s["so_done"], at.at("r", times=2) + (a + 1))
                hi, lo = tile(m.b_hi, i * 2 + a), tile(m.b_lo, i * 2 + a)
                own(ts(hi, m.bank[5][:], 1.0, None, ALU.mult))
                own(tt(lo, m.bank[5][:], hi.bitcast(F32), ALU.subtract))
                dve.sem_inc(s["so_free"], 1)
                dve.sem_inc(s["branch_b"], 1)

            def r_weights():
                dve.wait_ge(s["rs_done"], at.at("r", 1))
                dve.wait_ge(s["dec_in"], at.at("r", 1, times=16))
                for sb in range(TB):
                    n = S - sb * P
                    ins = tt(m.sp[:, SOFF[sb]:SOFF[sb] + n], st[sb], m.dec[:, 0:n], ALU.mult)
                ins.then_inc(s["rw_ready"], 1)

            def r_statistics():
                dve.wait_ge(s["rpv_done"], at.at("r", 1))
                for b in range(TB):
                    ins = nc.vector.bn_stats(m.sm[:, 12 + 6 * b:18 + 6 * b],
                                             m.bank[5 + b // 2][:, (b % 2) * R_DV:(b % 2) * R_DV + R_DV])
                own(ins)
                dve.sem_inc(s["stats_step"], 1)
                for b in range(TB):
                    ins = nc.vector.bn_aggr(m.sm[:, 56 + 2 * b:58 + 2 * b], m.sm[:, 12 + 6 * b:18 + 6 * b])
                ins.then_inc(s["var_ready"], 1)

            def r_normalised():
                dve.wait_ge(s["r_rstd_ready"], at.at("r", 1))
                for b in range(TB):
                    ins = ts(m.ro[:, b], m.bank[5 + b // 2][:, (b % 2) * R_DV:(b % 2) * R_DV + R_DV],
                             m.sm[:, 56 + 2 * b:57 + 2 * b], m.sm[:, 64 + b:65 + b], ALU.subtract, ALU.mult)
                ins.then_inc(s["ro_ready"], 1)

            def r_gate(half):
                dve.wait_ge(s["rsig_ready"], at.at("r", times=2) + (half + 1))
                c = take_panel()
                own(tt(m.rg[half][:], acc[c][:], m.rg[half][:], ALU.mult))
                dve.sem_inc(acc_free[c], 1)

            def r_branch(i, half):
                dve.wait_ge(s["roT_done"], at.at("r", times=2) + (half + 1))
                own(tt(m.rg[half][:], misc[:], m.rg[half][:], ALU.mult))
                dve.sem_inc(s["misc_free"], 1)
                split(tile(m.a_hi, i * 2 + half), tile(m.a_lo, i * 2 + half), m.rg[half][:], s["branch_a"])

            dve.wait_ge(s["const_in"], 16 * 5)
            dve.wait_ge(s["mask_in"], 16)
            for dst, src in ((m.ident_b, m.ident[:]), (m.mq_b, m.cst[:, C_MQ:C_MQ + P]),
                             (m.ms_b, m.cst[:, C_MS:C_MS + TB * P]), (m.mx_b, m.cst[:, C_MX:C_MX + P])):
                nc.vector.tensor_copy(dst[:], src).then_inc(s["masks_ready"], 1)
            dve.wait_ge(s["pos_in"], 16)
            own(nc.vector.tensor_copy(m.ang[:], m.posi[:]))
            own(ts(m.ang[:], m.ang[:], m.col[:, 0:1], None, ALU.mult))
            own(ts(m.turns[:], m.ang[:], 1.0 / (2 * math.pi), None, ALU.mult))
            own(nc.vector.tensor_copy(m.turni[:], m.turns[:]))
            own(nc.vector.tensor_copy(m.turns[:], m.turni[:]))
            own(stt(m.red[:], m.turns[:], -TWO_PI[0], m.ang[:], ALU.mult, ALU.add))
            own(stt(m.red[:], m.turns[:], -TWO_PI[1], m.red[:], ALU.mult, ALU.add))
            own(stt(m.red[:], m.turns[:], -TWO_PI[2], m.red[:], ALU.mult, ALU.add))

            def wrap(x):
                own(ts(m.turns[:], x[:], math.pi, -2 * math.pi, ALU.is_gt, ALU.mult))
                own(tt(x[:], x[:], m.turns[:], ALU.add))
                own(ts(m.turns[:], x[:], -math.pi, 2 * math.pi, ALU.is_lt, ALU.mult))
                own(tt(x[:], x[:], m.turns[:], ALU.add))

            wrap(m.red)
            own(ts(m.red2[:], m.red[:], math.pi / 2, None, ALU.add))
            wrap(m.red2)
            for x in (m.red, m.red2):
                ts(x[:], x[:], SIN_MAX, -SIN_MAX, ALU.min, ALU.max).then_inc(s["angles_ready"], 1)
            dve.wait_ge(s["sin_ready"], 1)
            own(ts(m.sin[:], m.sin[:], m.col[:, 1:2], None, ALU.mult))
            dve.wait_ge(s["x_in"], 16)
            dve.sem_inc(s["x_done"], KT)

            with at.loop(DEPTH, panel=PANELS_L1, acc=PANELS_L1 - PANELS_D, norm=1, proj4=2, layer=1, a=A_HEADS,
                         pair=B_HEADS // 2, u=KT, own=DVE_L1):
                norm()
                lambdas()
                take_panel()
                take_panel()
                take_panel()
                rotate_qk(0, 0)
                rotate_qk(1, 0)
                gate_rows()
                with at.loop(A_HEADS - 1, panel=4, acc=4, a=1, own=DVE_A) as i:
                    maxima()
                    combine()
                    take_panel()
                    take_panel()
                    take_panel()
                    rotate_qk(0, 1)
                    head_output()
                    rotate_qk(1, 1)
                    head_normalised()
                    head_gate()
                    head_branch(i)
                    at.add("a")
                maxima()
                combine()
                head_output()
                head_normalised()
                head_gate()
                head_branch(A_HEADS - 1)
                at.add("a")
                dve.wait_ge(s["rowsT_done"], at.at("layer", 1))
                cols_ps = misc[:, 0:64].rearrange("p (i b h) -> p i h b", i=2, h=B_HEADS)
                nc.vector.tensor_copy(m.gcol[:], cols_ps[:, 0])
                own(nc.vector.tensor_copy(m.ecol[:], cols_ps[:, 1]))
                dve.sem_inc(s["misc_free"], 1)
                for va in m.va:
                    nc.vector.memset(va[:, :, B_DV:B_DV + 1], 1.0)
                at.add("layer")

                with at.loop(B_HEADS // 2, panel=8, acc=8, pair=1, own=DVE_B) as j:
                    ts(m.pcol[:], m.gcol[:, bass.ds(j * 2, 2)], 1.0, None, ALU.mult).then_inc(s["pcol_ready"], 1)
                    convolve(m.yq, j, s["yq_ready"])
                    convolve(m.yk, j + 4, s["yk_ready"])
                    take_panel()
                    take_panel()
                    dve.wait_ge(s["bsig_ready"], at.at("pair", times=2) + 1)
                    own(stt(m.yq[:], m.yq[:], B_DK ** -0.5, m.sgq[:], ALU.mult, ALU.mult))
                    dve.wait_ge(s["bsig_ready"], at.at("pair", times=2) + 2)
                    tt(m.yk[:], m.yk[:], m.sgk[:], ALU.mult).then_inc(s["bqk_ready"], 1)
                    m_weights(0)
                    m_gate(0)
                    m_output(j, 0)
                    m_normalised(0)
                    m_weights(1)
                    m_branch(j, 0)
                    m_output(j, 1)
                    m_normalised(1)
                    m_gate(1)
                    m_branch(j, 1)
                    at.add("pair")
                merge()
                at.tiles = KT
                add_to_x()

            with at.loop(DEPTH, panel=PANELS_L2, acc=PANELS_L2 - PANELS_D - 2 * PANELS_DOWN, norm=2, proj4=6,
                         r=R_HEADS, u=KT, up=32, own=DVE_L2):
                norm()
                with at.loop(R_HEADS, panel=12, acc=12, r=1, own=DVE_R) as i:
                    at.add("panel", 6)
                    at.add("acc", 6)
                    softplus(0)
                    stick_branch(i, 0)
                    softplus(1)
                    at.add("panel", 4)
                    at.add("acc", 4)
                    dve.wait_ge(s["rotq2_in"], at.at("r", 1, times=32))
                    dve.wait_ge(s["table_in"], 32)
                    rotate(m.rq, m.rrq, m.cos, m.sin, None, None)
                    dve.wait_ge(s["rotk2_in"], at.at("r", 1, times=32))
                    rotate(m.rk, m.rrk, m.cos, m.sin, None, s["rqk_ready"])
                    stick_branch(i, 1)
                    r_weights()
                    r_gate(0)
                    r_statistics()
                    r_normalised()
                    r_gate(1)
                    r_branch(i, 0)
                    r_branch(i, 1)
                    at.add("r")
                merge()
                at.tiles = KT
                add_to_x()
                norm()
                with at.loop(2, panel=PANELS_UP + PANELS_DOWN, acc=16, up=16, proj4=2, own=16 + 2) as f:
                    with at.loop(4, panel=4, acc=4, up=4, own=4) as n:
                        for j in range(4):
                            dve.wait_ge(s["up_sq_ready"], at.at("up", 1))
                            take_panel()
                            split(tile(m.up_hi, n * 4 + j), tile(m.up_lo, n * 4 + j), m.mm[j % 2][:], s["up_ready"])
                            at.add("up")
                    at.tiles = 16
                    add_to_x()
            dve.wait_ge(s["rms_ready"], at.at("norm", 1))
            dve.wait_ge(s["gfin_in"], 16)
            for b in range(TB):
                own(ts(m.xn[:, b], m.x[:, b], m.sm[:, 4 + b:5 + b], None, ALU.mult))
                tt(m.xn[:, b], m.xn[:, b], m.g_fin[:], ALU.mult).then_inc(s["out_ready"], 1)


def kernel(**inputs):
    import concourse.bacc as bacc
    from concourse.bass_utils import run_bass_kernel_spmd

    nc = bacc.Bacc("TRN2", target_bir_lowering=False, num_devices=1)
    arrays, t = {}, {}
    for name, a in {**inputs, **constant_arrays()}.items():
        a = np.ascontiguousarray(a)
        arrays[f"in_{name}"] = a
        t[name] = nc.dram_tensor(f"in_{name}", a.shape, mybir.dt.from_np(a.dtype), kind="ExternalInput").ap()
    out = nc.dram_tensor("out_x", (1, S, D), F32, kind="ExternalOutput").ap()
    program(nc, t, out)
    r = run_bass_kernel_spmd(nc, [arrays], core_ids=[0])
    return r.results[0]["out_x"]
```

```python
import math
from contextlib import ExitStack, contextmanager

import numpy as np

import concourse.bass as bass
from concourse import mybir

F32 = mybir.dt.float32
F32R = mybir.dt.float32r
BF16 = mybir.dt.bfloat16
I32 = mybir.dt.int32
ACT = mybir.ActivationFunctionType
ALU = mybir.AluOpType
AX_X = mybir.AxisListType.X

P = 128
D = 1024
S = 512
DEPTH = 2
KT = D // P
TB = S // P
EPS = 1e-6
GN_EPS = 1e-5
BIG_NEG = -1e30

A_HEADS, A_DH, A_DV = 8, 64, 128
B_HEADS, B_DK, B_DV = 8, 64, 128
AQ, AK, AV, AZ, BQK, BV, BO, BZ, GA1, GB1 = (KT * i for i in range(10))
GATES = 6 * D
R_HEADS, R_DK, R_DV = 4, 128, 256
S_HEADS, S_DH = 8, 128
QR, KR, VR, GR, QS, KS, VS, GA2, GB2 = 0, 4, 8, 16, 24, 32, 40, 48, 56

QOFF = [0, 128, 384, 768]
SOFF = [0, 512, 1024, 896]
TRI = 1280

RING = 4
A_TAPS = 4

G_QK, G_B, BIASES, G_A, CONV_W, CONV_B, PRM_IN, LAM_INIT, G_A_SCALED, NEG_LAMBDA = 0, 2, 3, 4, 5, 37, 45, 45, 46, 47
PRM_DMAS = 4
TWO_PI = (6.28125, 0.0019340515136718750, 2 * math.pi - 6.28125 - 0.0019340515136718750)
SIN_MAX = 3.1415925

C_IDENT = 0
C_MQ = 128
C_MS = 256
C_MX = 768
C_GRP = 896
C_TRI = 1024
C_NEG1 = 1152
C_INVF = 1280
C_SGN = 1281
C_EPS = 1282
C_GEPS = 1283
C_ONE = 1284
CST = 1288


def constant_arrays():
    c = np.zeros((P, CST), np.float32)
    i = np.arange(P)
    c[:, C_IDENT:C_IDENT + P] = np.eye(P)
    c[:, C_MQ:C_MQ + P] = np.where(i[None, :] <= i[:, None], 0.0, BIG_NEG)
    key_major = np.where(i[:, None] <= i[None, :], 0.0, BIG_NEG)
    c[:, C_MS:C_MS + TB * P] = np.tile(key_major, (1, TB))
    c[:, C_MX:C_MX + P] = np.where(i[:, None] < i[None, :], 0.0, BIG_NEG)
    c[:, C_GRP:C_GRP + P] = (i[:, None] // 64 == i[None, :] // 64)
    c[:, C_TRI:C_TRI + P] = np.where(i[:, None] >= i[None, :], -1.0, 0.0)
    c[:, C_NEG1:C_NEG1 + P] = -1.0
    c[:, C_INVF] = 10000.0 ** (-2.0 * (i % 32) / A_DH)
    c[:, C_SGN] = np.where(i % 64 < 32, -1.0, 1.0)
    c[:, C_EPS] = EPS
    c[:, C_GEPS] = GN_EPS
    c[:, C_ONE] = 1.0
    inv = (10000.0 ** (-np.arange(64, dtype=np.float64) / 64)).astype(np.float32)
    ang = (np.arange(S, dtype=np.float32)[None, :] * inv[i % 64][:, None]).astype(np.float64)
    rot = np.stack([np.cos(ang), np.sin(ang) * np.where(i < 64, -1.0, 1.0)[:, None]], 1)
    gamma = 1.0 - 2.0 ** (-5.0 - np.arange(R_HEADS))
    diff = np.arange(S)[None, :] - i[:, None]
    dec = np.where(diff[None] >= 0, gamma[:, None, None] ** np.maximum(diff, 0)[None], 0.0)
    dec = (dec * R_DK ** -0.5).transpose(1, 0, 2)
    sel = np.zeros((B_HEADS, B_HEADS, P), np.float32)
    for h in range(B_HEADS):
        sel[h, h] = 1.0
    lam = np.array([[0.8 - 0.6 * math.exp(-0.3 * l)] for l in range(DEPTH)], np.float32)
    return {
        "cst": c,
        "rot2": rot.astype(np.float32),
        "decay": np.ascontiguousarray(dec.astype(np.float32)),
        "sel": sel,
        "lam_init": lam,
    }


class Place:

    def __init__(self, eng):
        self.eng, self.terms, self.n = eng, [], {}

    @contextmanager
    def loop(self, turns, **per):
        with self.eng.Fori(0, turns) as reg:
            start = dict(self.n)
            self.terms.append((reg, per))
            yield reg
            self.terms.pop()
        for k in set(self.n) | set(per):
            grew = self.n.get(k, 0) - start.get(k, 0)
            assert grew == per.get(k, 0), f"one turn adds {grew} to {k}, not {per.get(k, 0)}"
            self.n[k] = start.get(k, 0) + turns * per.get(k, 0)

    def add(self, name, k=1):
        self.n[name] = self.n.get(name, 0) + k
        return k

    def at(self, name, more=0, div=1, times=1):
        v = (self.n.get(name, 0) + more) // div * times
        for reg, per in self.terms:
            k = per.get(name, 0)
            assert k % div == 0, (name, k, div)
            if k:
                v = reg * (k // div * times) + v
        return v

    def slot(self, ring):
        return self.n.get("panel", 0) % ring


PANELS_A = A_HEADS * 4
PANELS_B = (B_HEADS // 2) * 8
PANELS_C = KT * 4
PANELS_D = 2 * 4
PANELS_R = R_HEADS * 12
PANELS_UP = 16
PANELS_DOWN = 2 * 8
PANELS_L1 = PANELS_A + PANELS_B + PANELS_C + PANELS_D
PANELS_L2 = PANELS_R + PANELS_C + PANELS_D + 2 * (PANELS_UP + PANELS_DOWN)


PE_MISC_L1 = 50
PE_MISC_L2 = 20
ACT_L1 = 133
ACT_A = 8
ACT_B = 10
ACT_L2 = 112
ACT_R = 11
DVE_L1 = 359
DVE_A = 25
DVE_B = 28
DVE_L2 = 196
DVE_R = 33


class Region:

    def __init__(self, nc, start, end):
        self.nc, self.cursor, self.end = nc, start, end

    def put(self, name, shape, dt=F32):
        size = int(np.prod(shape[1:])) * (2 if dt == BF16 else 4)
        buf = self.nc.alloc_sbuf_tensor_at(name, shape, dt, offset=self.cursor)
        self.cursor += (size + 31) // 32 * 32
        assert self.cursor <= self.end, (name, self.cursor - self.end)
        return buf


class Memory:

    def __init__(self, nc, ctx):
        tile = KT * S * 4
        base = (nc.sbuf_base + 31) // 32 * 32
        o_x = base
        o_h = o_x + tile
        o_a = o_h + 2 * tile
        o_b = o_a + 2 * tile
        o_w = o_b + 2 * tile
        o_u = o_w + 2 * RING * KT * P * 4
        o_rest = o_u + 3 * tile

        kts, kw = [P, KT, S], [P, RING, KT * P]
        place = Region(nc, o_x, o_h)
        self.x = place.put("x", [P, TB, D])
        place = Region(nc, o_h, o_a)
        self.h_hi = place.put("h_hi", kts, F32R)
        self.h_lo = place.put("h_lo", kts, F32R)
        place = Region(nc, o_a, o_b)
        self.a_hi = place.put("a_hi", kts, F32R)
        self.a_lo = place.put("a_lo", kts, F32R)
        place = Region(nc, o_b, o_w)
        self.b_hi = place.put("b_hi", kts, F32R)
        self.b_lo = place.put("b_lo", kts, F32R)
        place = Region(nc, o_w, o_u)
        self.raw = place.put("raw", kw)
        self.w_hi = place.put("w_hi", kw, F32R)
        place = Region(nc, o_w, o_u)
        self.w_lo = place.put("w_lo", kw, F32R)
        place = Region(nc, o_u, o_rest)
        self.u_hi = place.put("u_hi", kts, F32R)
        self.u_lo = place.put("u_lo", kts, F32R)
        place = Region(nc, o_rest, nc.sbuf_top)
        self.ident = place.put("ident", [P, P])
        self.grp = place.put("grp", [P, P], F32R)
        self.ntri = place.put("ntri", [P, P], F32R)
        self.neg1 = place.put("neg1", [P, P], F32R)
        self.col = place.put("col", [P, 8])
        self.ident_b = place.put("ident_b", [P, P], BF16)
        self.mq_b = place.put("mq_b", [P, P], BF16)
        self.mx_b = place.put("mx_b", [P, P], BF16)
        self.ms_b = place.put("ms_b", [P, TB * P], BF16)
        self.g_norm = place.put("g_norm", [P, KT])
        self.prm = place.put("prm", [P, 48])
        self.sm = place.put("sm", [P, 96])
        self.gcol = place.put("gcol", [P, B_HEADS, TB])
        self.ecol = place.put("ecol", [P, B_HEADS, TB])
        self.pcol = place.put("pcol", [P, 2, TB])
        end = place.cursor
        place = Region(nc, end, nc.sbuf_top)
        self.cos = place.put("cos", [P, S])
        self.sin = place.put("sin", [P, S])
        at_cos = place.cursor
        place = Region(nc, at_cos, nc.sbuf_top)
        self.negg = place.put("negg", [8, S])
        self.negg_hi = place.put("negg_hi", [8, S], F32R)
        self.selp = place.put("selp", [8, 2, P])
        self.selp_r = place.put("selp_r", [8, 2, P], F32R)
        place = Region(nc, at_cos, nc.sbuf_top)
        self.negg_lo = place.put("negg_lo", [8, S], F32R)
        place = Region(nc, at_cos, nc.sbuf_top)
        self.sig_a = place.put("sig_a", [P, S])
        self.sig_b = place.put("sig_b", [P, S])
        place = Region(nc, at_cos, nc.sbuf_top)
        self.sp = place.put("sp", [P, TRI])
        self.stk_lo = place.put("stk_lo", [P, S], F32R)
        place = Region(nc, at_cos, nc.sbuf_top)
        self.sp_lo = place.put("sp_lo", [P, TRI], F32R)
        place = Region(nc, o_u, o_rest)
        self.xn = place.put("xn", [P, TB, D])
        place = Region(nc, o_h, o_a)
        self.junk = place.put("junk", [P, TB, 512])
        self.g_fin = place.put("g_fin", [P, D])
        place = Region(nc, o_a, o_b)
        self.cst = place.put("cst", [P, CST])
        place = Region(nc, o_b, o_w)
        self.posi = place.put("posi", [P, S], I32)
        self.ang = place.put("ang", [P, S])
        self.turns = place.put("turns", [P, S])
        self.turni = place.put("turni", [P, S], I32)
        self.red = place.put("red", [P, S])
        self.red2 = place.put("red2", [P, S])
        place = Region(nc, o_b, o_w)
        self.wif = place.put("wif", [P, KT, 16])
        self.wif_hi = place.put("wif_hi", [P, KT, 16], F32R)
        self.wif_lo = place.put("wif_lo", [P, KT, 16], F32R)
        self.lqk = place.put("lqk", [P, 4, A_DH])
        self.lqp = place.put("lqp", [P, 2, A_DH])
        self.g16 = place.put("g16", [16, S])
        self.frow = place.put("frow", [8, S])
        self.lrow = place.put("lrow", [8, S])
        self.fcum = place.put("fcum", [8, S])
        self.grow = place.put("grow", [8, S])
        self.erow = place.put("erow", [8, S])
        self.zrow = place.put("zrow", [8, S])
        self.p0 = place.put("p0", [P, TRI])
        self.p1 = place.put("p1", [P, TRI])
        self.sqh_q = place.put("sqh_q", [P, S], F32R)
        self.sqh_k = place.put("sqh_k", [P, S], F32R)
        place = Region(nc, o_u, o_rest)
        self.xq = place.put("xq", [P, S])
        self.xk = place.put("xk", [P, S])
        self.sq_q = place.put("sq_q", [P, S])
        self.sq_k = place.put("sq_k", [P, S])
        self.rot_q = place.put("rot_q", [P, S])
        self.rot_k = place.put("rot_k", [P, S])
        self.vT = place.put("vT", [P, S])
        self.v = place.put("v", [P, TB, A_DV])
        self.sg = place.put("sg", [P, S])
        self.sz = place.put("sz", [P, S])
        self.o_sb = place.put("o_sb", [P, TB, A_DV])
        self.o_sq = place.put("o_sq", [P, TB, A_DV])
        self.q_hi = place.put("q_hi", [P, S], F32R)
        self.q_lo = place.put("q_lo", [P, S], F32R)
        self.k_hi = place.put("k_hi", [P, S], F32R)
        self.k_lo = place.put("k_lo", [P, S], F32R)
        place = Region(nc, o_u, o_rest)
        self.yq = place.put("yq", [P, S])
        self.yk = place.put("yk", [P, S])
        self.sgq = place.put("sgq", [P, S])
        self.sgk = place.put("sgk", [P, S])
        self.vTb = place.put("vTb", [P, S])
        self.va0 = place.put("va0", [P, TB, B_DV + 4])
        self.va1 = place.put("va1", [P, TB, B_DV + 4])
        self.e = place.put("e", [P, TRI])
        self.hs = place.put("hs", [P, TB, B_DV])
        self.h_sq = place.put("h_sq", [P, TB, B_DV])
        self.og = place.put("og", [P, S])
        self.zg = place.put("zg", [P, S])
        self.gate = place.put("gate", [P, S])
        place = Region(nc, o_u, o_rest)
        self.stq_hi = place.put("stq_hi", [P, S], F32R)
        self.stk_hi = place.put("stk_hi", [P, S], F32R)
        self.svT = place.put("svT", [P, S])
        self.sv_hi = place.put("sv_hi", [P, TB, S_DH], F32R)
        self.rq = place.put("rq", [P, S])
        self.rk = place.put("rk", [P, S])
        self.rrq = place.put("rrq", [P, S])
        self.rrk = place.put("rrk", [P, S])
        self.rvT0 = place.put("rvT0", [P, S])
        self.rvT1 = place.put("rvT1", [P, S])
        self.rv_hi = place.put("rv_hi", [P, TB, R_DV], F32R)
        self.dec = place.put("dec", [P, S])
        self.rg0 = place.put("rg0", [P, S])
        self.rg1 = place.put("rg1", [P, S])
        self.stq_lo = place.put("stq_lo", [P, S], F32R)
        self.sv_lo = place.put("sv_lo", [P, TB, S_DH], F32R)
        self.rv_lo = place.put("rv_lo", [P, TB, R_DV], F32R)
        self.sw_hi = place.put("sw_hi", [P, TRI], F32R)
        place = Region(nc, o_u + 4 * S * 4, o_rest)
        self.ro = place.put("ro", [P, TB, R_DV])
        place = Region(nc, o_u + 8 * S * 4, o_rest)
        self.sp_hi = place.put("sp_hi", [P, TRI], F32R)
        place = Region(nc, o_a, o_w)
        self.up_hi = place.put("up_hi", [P, 16, S], F32R)
        self.up_lo = place.put("up_lo", [P, 16, S], F32R)
        place = Region(nc, o_u, o_rest)
        self.m0 = place.put("m0", [P, S])
        self.m1 = place.put("m1", [P, S])
        self.mm0 = place.put("mm0", [P, S])
        self.mm1 = place.put("mm1", [P, S])
        place = Region(nc, o_u + 2 * S * 4, o_rest)
        self.sql_q = place.put("sql_q", [P, S], F32R)
        self.sql_k = place.put("sql_k", [P, S], F32R)
        place = Region(nc, o_u, o_rest)
        self.yq_lo = place.put("yq_lo", [P, S], F32R)
        self.yk_lo = place.put("yk_lo", [P, S], F32R)
        self.yq_hi = place.put("yq_hi", [P, S], F32R)
        self.yk_hi = place.put("yk_hi", [P, S], F32R)
        place = Region(nc, o_u + 4 * S * 4, o_rest)
        self.rq_lo = place.put("rq_lo", [P, S], F32R)
        self.rk_lo = place.put("rk_lo", [P, S], F32R)
        self.rq_hi = place.put("rq_hi", [P, S], F32R)
        self.rk_hi = place.put("rk_hi", [P, S], F32R)
        self.va = [self.va0, self.va1]
        self.rvT, self.rg = [self.rvT0, self.rvT1], [self.rg0, self.rg1]
        self.m, self.mm = [self.m0, self.m1], [self.mm0, self.mm1]
        self.bank = [ctx.enter_context(nc.psum_tensor(f"bank{i}", [P, 512], F32)) for i in range(8)]


SEMAPHORES = """
raw_in0 raw_in1 raw_in2 raw_in3 acc_free0 acc_free1 split out_ready out_done used w_step pv_done h_ready
misc_free xn_ready xT_done sq_ready ss_done vT_ready vT_done qk_ready scores_done a_ready p_ready turned
v_ready aT_ready on_ready oT_done wif_ready gates_done rows_ready erow_ready pe_step rowsT_done sel_in
hs_ready gb_done bqk_ready bs_done bvT_ready bvT_done bw_ready bv_ready bpv_done bon_ready boT_done sk_ready
z_done svT_ready svT_done sp_ready c_done sw_ready sv_ready so_free so_done rvT_ready rvT_done rqk_ready
rs_done rw_ready rv_ready rpv_done ro_ready roT_done branch_a branch_b u_ready const_in masks_ready up_ready
act_step x_done gain_in rms_ready h_hi_ready prm_in rstd_ready max_ready o_rstd_ready f_in row_ln_ready
rows_m_ready bsig_ready pcol_ready e_ready b_rstd_ready gate_ready og_ready ln_ready sA_ready sB_ready mask_in
pos_in angles_ready sin_ready lam_sum lam_exp rot_q_in rot_k_in sig_ready yq_ready yk_ready zg_ready table_in
dec_in rotq2_in rotk2_in rsig_ready var_ready r_rstd_ready up_sq_ready gfin_in dve_step stats_step x_in0 x_in1
x_in2 x_in3 xb_done bank2_free sel_ready stq_ready sk_lo_ready exp_ready sv_hi_ready
rv_hi_ready sq_split
""".split()


def program(nc, t, out):
    ctx = ExitStack()
    with ctx:
        m = Memory(nc, ctx)
        s = {name: ctx.enter_context(nc.semaphore(name)) for name in SEMAPHORES}
        x_in = [s[f"x_in{b}"] for b in range(TB)]
        raw_in = [s[f"raw_in{i}"] for i in range(RING)]
        acc_free = [s["acc_free0"], s["acc_free1"]]
        acc = [m.bank[0], m.bank[1]]
        misc = m.bank[7]
        st = [m.bank[2][:, 0:512], m.bank[3][:, 0:384], m.bank[4][:, 0:256], m.bank[3][:, 384:512]]
        mst = [m.bank[4][:, 0:512], m.bank[5][:, 0:384], m.bank[6][:, 0:256], m.bank[5][:, 384:512]]
        sq = [[m.bank[4 + k][:, 384:512], m.bank[6][:, 256 * k:256 * k + 256], m.bank[4 + k][:, 0:384],
               m.bank[2 + k][:, 0:512]] for k in range(2)]
        groups = ((0, 1), (2,), (3,))
        order = (1, 0, 2, 3)
        turn = [m.bank[6][:, 0:384], m.bank[4][:, 0:384], m.bank[2][:, 0:512]]
        pv = m.bank[3]
        xb = [m.bank[2 + i] for i in range(TB)]
        block = ctx.enter_context(nc.Block())

        @block.sync
        def _(sp):
            at = Place(sp)

            def panel(w, l, n):
                slot = at.slot(RING)
                sp.wait_ge(s["used"], at.at("panel", 1))
                sp.dma_start(m.raw[:, slot], t[w][bass.ds(l, 1), bass.ds(n, 1)].squeeze(0).squeeze(0)
                             ).then_inc(raw_in[slot], 16)
                at.add("panel")

            def merge(l, gates, ga, gb, wa, wb):
                with at.loop(KT, panel=4) as n:
                    panel(gates, l, n + ga)
                    panel(wa, l, n)
                    panel(gates, l, n + gb)
                    panel(wb, l, n)

            def project(l, w):
                with at.loop(2, panel=4) as c:
                    for q in range(KT // 2):
                        panel(w, l, c * (KT // 2) + q)

            sp.wait_ge(s["pos_in"], 16)
            sp.wait_ge(s["const_in"], 16 * 2)
            for b in range(TB):
                sp.dma_start(m.x[:, b], t["x"].rearrange("b (t p) d -> p (b t) d", p=P)[:, b]).then_inc(x_in[b], 16)
            sp.dma_start(m.cst[:, C_MQ:C_NEG1 + P], t["cst"][:, C_MQ:C_NEG1 + P]).then_inc(s["mask_in"], 16)
            with at.loop(DEPTH, panel=PANELS_L1) as l:
                panel("w_in", l, AQ)
                panel("w_in", l, AK)
                panel("w_in", l, AV)
                with at.loop(A_HEADS - 1, panel=4) as i:
                    panel("w_in", l, i + (AQ + 1))
                    panel("w_in", l, i + (AK + 1))
                    panel("w_in", l, i + (AV + 1))
                    panel("w_in", l, i + AZ)
                panel("w_in", l, AZ + A_HEADS - 1)
                with at.loop(B_HEADS // 2, panel=8) as j:
                    panel("w_in", l, j + BQK)
                    panel("w_in", l, j + (BQK + B_HEADS // 2))
                    panel("w_in", l, j * 2 + BV)
                    panel("w_in", l, j * 2 + (BV + 1))
                    for a in range(2):
                        panel("w_in", l, j * 2 + (BO + a))
                        panel("w_in", l, j * 2 + (BZ + a))
                merge(l, "w_in", GA1, GB1, "w_out_a", "w_out_b")
                project(l, "w_o")
            with at.loop(DEPTH, panel=PANELS_L2) as l:
                with at.loop(R_HEADS, panel=12) as i:
                    for a in range(2):
                        panel("w_in_2", l, i * 2 + (QS + a))
                        panel("w_in_2", l, i * 2 + (KS + a))
                        panel("w_in_2", l, i * 2 + (VS + a))
                    panel("w_in_2", l, i + QR)
                    panel("w_in_2", l, i + KR)
                    for half in range(2):
                        panel("w_in_2", l, i * 2 + (VR + half))
                    for half in range(2):
                        panel("w_in_2", l, i * 2 + (GR + half))
                merge(l, "w_in_2", GA2, GB2, "p_ret_2", "p_sb_2")
                project(l, "w_out_2")
                with at.loop(2, panel=PANELS_UP + PANELS_DOWN) as f:
                    with at.loop(4, panel=4) as n:
                        for j in range(4):
                            panel("w_up_2", l, f * 16 + n * 4 + j)
                    with at.loop(2, panel=8) as c:
                        for q in range(8):
                            panel("w_down_2", l, c * 16 + f * 8 + q)
            for b in range(TB):
                sp.wait_ge(s["out_ready"], b + 1)
                sp.dma_start(out.rearrange("b (t p) d -> p (b t) d", p=P)[:, b],
                             m.xn[:, b]).then_inc(s["out_done"], 16)
            sp.wait_ge(s["out_done"], 16 * TB)
            for i in range(RING):
                sp.wait_ge(raw_in[i], at.at("panel", div=RING, times=16))

        @block.gpsimd
        def _(pool):
            at = Place(pool)

            def split_panel():
                slot = at.slot(RING)
                pool.wait_ge(raw_in[slot], at.at("panel", RING, div=RING, times=16))
                pool.sem_inc(s["w_step"], 1)
                nc.gpsimd.tensor_scalar(m.w_hi[:, slot], m.raw[:, slot], 1.0, 0.0, ALU.mult,
                                        ALU.add).then_inc(s["w_step"], 1)
                pool.wait_ge(s["w_step"], at.at("panel", 1, times=2))
                nc.gpsimd.tensor_tensor(m.w_lo[:, slot], m.raw[:, slot], m.w_hi[:, slot].bitcast(F32),
                                        ALU.subtract).then_inc(s["split"], 1)
                at.add("panel")

            with at.loop((DEPTH * (PANELS_L1 + PANELS_L2)) // RING, panel=RING):
                for _ in range(RING):
                    split_panel()

        @block.tensor
        def _(pe):
            at = Place(pe)
            pe.sem_inc(s["used"], RING)
            pe.sem_inc(s["pv_done"], 1)

            def product(dst, hi, lo, rhs_hi, rhs_lo, first, last, **more):
                nc.tensor.matmul(dst, hi, rhs_lo, start=first, stop=False, **more)
                nc.tensor.matmul(dst, lo, rhs_hi, start=False, stop=False, **more)
                return nc.tensor.matmul(dst, hi, rhs_hi, start=False, stop=last, **more)

            def gemm(x_hi, x_lo, fresh=False):
                slot = at.slot(RING)
                c = at.n.get("acc", 0) % 2
                pe.wait_ge(s["split"], at.at("panel", 1))
                pe.wait_ge(acc_free[c], at.at("acc", 2, div=2))
                for k in range(KT):
                    if fresh:
                        pe.wait_ge(s["h_ready"], at.at("norm", -1, times=KT) + (k + 1))
                    w = slice(k * P, k * P + P)
                    mm = product(acc[c][:], m.w_hi[:, slot, w], m.w_lo[:, slot, w], x_hi[:, k], x_lo[:, k],
                                 k == 0, k == KT - 1)
                mm.then_inc(s["used"], 1)
                at.add("panel")
                at.add("acc")

            def project(x_hi, x_lo, tiles, ready, before):
                for q in range(tiles // 2):
                    slot = at.slot(RING)
                    pe.wait_ge(s["split"], at.at("panel", 1))
                    pe.wait_ge(s[ready], before + (2 * q + 2))
                    for b in range(TB):
                        tok = slice(b * P, b * P + P)
                        if q == 0:
                            pe.wait_ge(s["x_done"], at.at("xb", times=TB) + (TB + b + 1))
                        for k in range(2):
                            w = slice(k * 512, k * 512 + 512)
                            kt = 2 * q + k
                            mm = product(xb[b][:], x_hi[:, kt, tok], x_lo[:, kt, tok], m.w_hi[:, slot, w],
                                         m.w_lo[:, slot, w], kt == 0, kt == tiles - 1)
                        if q == tiles // 2 - 1 and b < TB - 1:
                            mm.then_inc(s["xb_done"], 1)
                    mm.then_inc(s["used"], 1)
                    at.add("panel")
                at.add("xb")

            def misc_bank():
                pe.wait_ge(s["misc_free"], at.at("misc", 1))
                at.add("misc")

            def norm_turns():
                def turn_block(k, b):
                    return nc.tensor.transpose(xb[k % TB][:, b * P:b * P + P], m.xn[:, b, k * P:k * P + P],
                                               m.ident[:])

                for b in range(TB):
                    pe.wait_ge(s["xn_ready"], at.at("norm", times=TB) + (b + 1))
                    for k in range(TB):
                        mm = turn_block(k, b)
                        if b == TB - 1:
                            mm.then_inc(s["xT_done"], 1)
                for k in range(TB, KT):
                    pe.wait_ge(s["h_ready"], at.at("norm", times=KT) + (k - TB + 1))
                    for b in range(TB):
                        mm = turn_block(k, b)
                    mm.then_inc(s["xT_done"], 1)

            def turn4(dst, src):
                for b in range(TB):
                    mm = nc.tensor.transpose(dst[:, b * P:b * P + P], src(b), m.ident[:])
                return mm

            def group_sum(which, ahead):
                lo, hi = ((m.sql_q, m.sqh_q), (m.sql_k, m.sqh_k))[which]
                pe.wait_ge(s["sq_split"], at.at("a", ahead, times=2) + (which + 1))
                misc_bank()
                nc.tensor.matmul(misc[:], m.grp[:], lo[:], start=True, stop=False)
                nc.tensor.matmul(misc[:], m.grp[:], hi[:], start=False, stop=True).then_inc(s["ss_done"], 1)

            def value_turns(ahead):
                pe.wait_ge(s["vT_ready"], at.at("a", ahead + 1))
                misc_bank()
                turn4(misc, lambda b: m.vT[:, b * P:b * P + P]).then_inc(s["vT_done"], 1)

            def scores():
                pe.wait_ge(s["qk_ready"], at.at("a", 1, times=2))
                pe.wait_ge(s["on_ready"], at.at("a", 1))
                for k in range(2):
                    r = slice(64 * k, 64 * k + 64)
                    for qb in ((1, 3, 2, 0), (3, 2, 1, 0))[k]:
                        if (k, qb) == (1, 1):
                            pe.wait_ge(s["scores_done"], at.at("a", times=2) + 1)
                        tok, keys = slice(qb * P, qb * P + P), slice(0, (qb + 1) * P)
                        product(sq[k][qb], m.q_hi[r, tok], m.q_lo[r, tok], m.k_hi[r, keys], m.k_lo[r, keys],
                                True, False)
                        mm = nc.tensor.matmul(sq[k][qb][:, qb * P:qb * P + P], m.ident_b[:], m.mq_b[:],
                                              start=False, stop=True)
                        if (k, qb) in ((0, 1), (1, 0)):
                            mm.then_inc(s["scores_done"], 1)

            def weight_turns(g):
                pe.wait_ge(s["a_ready"], at.at("a", times=TB) + (g + 2))
                start = QOFF[groups[g][0]]
                for qb in groups[g]:
                    for sb in range(qb + 1):
                        o = QOFF[qb] + sb * P
                        mm = nc.tensor.transpose(turn[g][:, o - start:o - start + P], m.p0[:, o:o + P], m.ident[:])
                mm.then_inc(s["turned"], 1)

            def values(g):
                if g == 0:
                    pe.wait_ge(s["v_ready"], at.at("a", 1))
                    pe.wait_ge(s["p_ready"], at.at("a", times=TB) + TB)
                pe.wait_ge(s["aT_ready"], at.at("a", times=len(groups)) + (g + 1))
                for qb in groups[g]:
                    for sb in range(qb + 1):
                        o = QOFF[qb] + sb * P
                        mm = nc.tensor.matmul(pv[:, qb * P:qb * P + P], m.p1[:, o:o + P], m.v[:, sb],
                                              start=sb == 0, stop=sb == qb)
                if g == len(groups) - 1:
                    mm.then_inc(s["pv_done"], 1)

            def output_turns():
                pe.wait_ge(s["on_ready"], at.at("a", 2))
                misc_bank()
                turn4(misc, lambda b: m.o_sb[:, b]).then_inc(s["oT_done"], 1)

            def h_gemm():
                gemm(m.h_hi, m.h_lo)

            def gate_rows():
                pe.wait_ge(s["wif_ready"], at.at("layer", 1))
                misc_bank()
                for k in range(KT):
                    mm = product(misc[0:16, :], m.wif_hi[:, k], m.wif_lo[:, k], m.h_hi[:, k], m.h_lo[:, k],
                                 k == 0, k == KT - 1)
                mm.then_inc(s["gates_done"], 1)

            def row_turns():
                pe.wait_ge(s["rows_ready"], at.at("layer", 1))
                pe.wait_ge(s["erow_ready"], at.at("layer", 1))
                misc_bank()
                pe.sem_inc(s["pe_step"], 1)
                for i, row in enumerate((m.grow, m.erow)):
                    for b in range(TB):
                        mm = nc.tensor.transpose(misc[:, (i * TB + b) * 8:(i * TB + b) * 8 + 8],
                                                 row[:, b * P:b * P + P], m.ident[0:8, 0:8])
                mm.then_inc(s["rowsT_done"], 1)

            def spread_gate(a):
                pe.wait_ge(s["sel_ready"], at.at("pair", 1))
                pe.wait_ge(s["hs_ready"], at.at("pair", times=2) + (a + 1))
                for bank in (2, 3):
                    nc.tensor.matmul(m.bank[bank][:], m.selp_r[:, a], m.negg_lo[:], start=True, stop=False)
                    nc.tensor.matmul(m.bank[bank][:], m.selp_r[:, a], m.negg_hi[:], start=False, stop=bank == 2)
                nc.tensor.matmul(m.bank[3][:], m.ident_b[:], m.ms_b[:], start=False,
                                 stop=True).then_inc(s["gb_done"], 1)

            def m_scores(a):
                if a == 0:
                    pe.wait_ge(s["bqk_ready"], at.at("pair", 1, times=2))
                r = slice(64 * a, 64 * a + 64)
                for sb in range(TB):
                    keys, tok = slice(sb * P, sb * P + P), slice(sb * P, S)
                    mm = product(mst[sb], m.yk_hi[r, keys], m.yk_lo[r, keys], m.yq_hi[r, tok], m.yq_lo[r, tok],
                                 True, True)
                mm.then_inc(s["bs_done"], 1)

            def m_value_turns(a):
                pe.wait_ge(s["bvT_ready"], at.at("pair", times=2) + (a + 1))
                misc_bank()
                turn4(misc, lambda b: m.vTb[:, b * P:b * P + P]).then_inc(s["bvT_done"], 1)

            def m_values(a):
                pe.wait_ge(s["bw_ready"], at.at("pair", times=2) + (a + 1))
                pe.wait_ge(s["bv_ready"], at.at("pair", times=2) + (a + 1))
                for qb in range(TB):
                    o = (qb % 2) * (B_DV + 4)
                    for sb in range(qb + 1):
                        w = SOFF[sb] + (qb - sb) * P
                        mm = nc.tensor.matmul(m.bank[2 + qb // 2][:, o:o + B_DV + 1], m.e[:, w:w + P],
                                              m.va[a][:, sb, 0:B_DV + 1], start=sb == 0, stop=sb == qb)
                mm.then_inc(s["bpv_done"], 1)

            def m_output_turns(a):
                pe.wait_ge(s["bon_ready"], at.at("pair", times=2) + (a + 1))
                misc_bank()
                turn4(misc, lambda b: m.hs[:, b]).then_inc(s["boT_done"], 1)

            def z_scores(a):
                pe.wait_ge(s["sk_lo_ready"], at.at("r", times=2) + (a + 1))
                if a == 0:
                    pe.wait_ge(s["bank2_free"], at.at("r", 1))
                for sb in range(TB):
                    keys, tok = slice(sb * P, sb * P + P), slice(sb * P, S)
                    product(st[sb], m.stk_hi[:, keys], m.stk_lo[:, keys], m.stq_hi[:, tok], m.stq_lo[:, tok],
                            sb < TB - 1, False, skip_group_check=True)
                    mm = nc.tensor.matmul(st[sb][:, 0:P], m.ident_b[:], m.mx_b[:], start=False, stop=True,
                                          skip_group_check=True)
                mm.then_inc(s["z_done"], 1)

            def s_value_turns(a):
                pe.wait_ge(s["svT_ready"], at.at("r", times=2) + (a + 1))
                misc_bank()
                turn4(misc, lambda b: m.svT[:, b * P:b * P + P]).then_inc(s["svT_done"], 1)

            def stick_sums(a):
                pe.wait_ge(s["sp_ready"], at.at("r", times=2) + (a + 1))
                for sb in range(TB):
                    n = S - sb * P
                    for sp in (m.sp_lo, m.sp_hi):
                        mm = nc.tensor.matmul(st[sb], m.ntri[:], sp[:, SOFF[sb]:SOFF[sb] + n],
                                              start=False, stop=True, skip_group_check=True)
                    for later in range(sb + 1, TB):
                        n = S - later * P
                        for sp in (m.sp_lo, m.sp_hi):
                            mm = nc.tensor.matmul(st[sb][:, (later - sb) * P:], m.neg1[:],
                                                  sp[:, SOFF[later]:SOFF[later] + n],
                                                  start=False, stop=True, skip_group_check=True)
                mm.then_inc(s["c_done"], 1)

            def s_values(a):
                pe.wait_ge(s["sw_ready"], at.at("r", times=2) + (a + 1))
                pe.wait_ge(s["sv_ready"], at.at("r", times=2) + (a + 1))
                pe.wait_ge(s["so_free"], at.at("r", times=2) + (a + 1))
                for sb in range(TB):
                    n = S - sb * P
                    w = slice(SOFF[sb], SOFF[sb] + n)
                    mm = product(m.bank[5][:, sb * P:S], m.sv_hi[:, sb], m.sv_lo[:, sb], m.sw_hi[:, w],
                                 m.sp_lo[:, w], sb == 0, sb == TB - 1)
                mm.then_inc(s["so_done"], 1)

            def r_value_turns(half):
                pe.wait_ge(s["rvT_ready"], at.at("r", times=2) + (half + 1))
                misc_bank()
                turn4(misc, lambda b: m.rvT[half][:, b * P:b * P + P]).then_inc(s["rvT_done"], 1)

            def r_scores():
                pe.wait_ge(s["rqk_ready"], at.at("r", 1, times=2))
                for sb in range(TB):
                    keys, tok = slice(sb * P, sb * P + P), slice(sb * P, S)
                    mm = product(st[sb], m.rk_hi[:, keys], m.rk_lo[:, keys], m.rq_hi[:, tok], m.rq_lo[:, tok],
                                 True, True)
                mm.then_inc(s["rs_done"], 1)

            def r_values():
                pe.wait_ge(s["rw_ready"], at.at("r", 2))
                pe.wait_ge(s["rv_ready"], at.at("r", 1, times=2))
                for qb in range(TB):
                    o = (qb % 2) * R_DV
                    for sb in range(qb + 1):
                        w = SOFF[sb] + (qb - sb) * P
                        mm = product(m.bank[5 + qb // 2][:, o:o + R_DV], m.sw_hi[:, w:w + P], m.sp_lo[:, w:w + P],
                                     m.rv_hi[:, sb], m.rv_lo[:, sb], sb == 0, sb == qb)
                mm.then_inc(s["rpv_done"], 1)

            def r_output_turns(half):
                if half == 0:
                    pe.wait_ge(s["ro_ready"], at.at("r", 1))
                    misc_bank()
                turn4((misc, m.bank[2])[half], lambda b: m.ro[:, b, half * P:half * P + P]).then_inc(s["roT_done"], 1)

            def merge():
                with at.loop(KT, panel=4, acc=4):
                    h_gemm()
                    pe.wait_ge(s["branch_a"], at.at("merge", 1, times=KT))
                    gemm(m.a_hi, m.a_lo)
                    h_gemm()
                    pe.wait_ge(s["branch_b"], at.at("merge", 1, times=KT))
                    gemm(m.b_hi, m.b_lo)
                at.add("merge")

            def project_merged():
                with at.loop(2, panel=4, xb=1):
                    project(m.u_hi, m.u_lo, KT, "u_ready", at.at("merge", -1, times=KT) + 1)

            def norm():
                norm_turns()

            pe.wait_ge(s["const_in"], 16 * 2)
            pe.wait_ge(s["masks_ready"], 7)
            with at.loop(DEPTH, panel=PANELS_L1, acc=PANELS_L1 - PANELS_D, xb=2, norm=1, layer=1, merge=1,
                         a=A_HEADS, pair=B_HEADS // 2, misc=PE_MISC_L1):
                norm()
                at.add("norm")
                gemm(m.h_hi, m.h_lo, fresh=True)
                h_gemm()
                group_sum(0, 0)
                h_gemm()
                group_sum(1, 0)
                value_turns(0)
                gate_rows()
                with at.loop(A_HEADS - 1, panel=4, acc=4, a=1, misc=4):
                    scores()
                    h_gemm()
                    weight_turns(0)
                    h_gemm()
                    group_sum(0, 1)
                    weight_turns(1)
                    values(0)
                    weight_turns(2)
                    h_gemm()
                    group_sum(1, 1)
                    values(1)
                    values(2)
                    value_turns(1)
                    h_gemm()
                    output_turns()
                    at.add("a")
                scores()
                h_gemm()
                for g in range(len(groups)):
                    weight_turns(g)
                for g in range(len(groups)):
                    values(g)
                row_turns()
                output_turns()
                at.add("a")

                at.add("layer")
                with at.loop(B_HEADS // 2, panel=8, acc=8, pair=1, misc=4):
                    h_gemm()
                    h_gemm()
                    h_gemm()
                    spread_gate(0)
                    h_gemm()
                    m_value_turns(0)
                    h_gemm()
                    m_scores(0)
                    m_value_turns(1)
                    h_gemm()
                    m_values(0)
                    m_scores(1)
                    spread_gate(1)
                    h_gemm()
                    m_output_turns(0)
                    m_values(1)
                    h_gemm()
                    m_output_turns(1)
                    at.add("pair")
                merge()
                project_merged()
            with at.loop(DEPTH, panel=PANELS_L2, acc=PANELS_L2 - PANELS_D - 2 * PANELS_DOWN, xb=6, norm=2,
                         merge=1, r=R_HEADS, half=2, misc=PE_MISC_L2):
                norm()
                at.add("norm")
                with at.loop(R_HEADS, panel=12, acc=12, r=1, misc=5):
                    gemm(m.h_hi, m.h_lo, fresh=True)
                    h_gemm()
                    h_gemm()
                    z_scores(0)
                    h_gemm()
                    s_value_turns(0)
                    h_gemm()
                    stick_sums(0)
                    h_gemm()
                    s_values(0)
                    z_scores(1)
                    h_gemm()
                    s_value_turns(1)
                    h_gemm()
                    stick_sums(1)
                    h_gemm()
                    s_values(1)
                    h_gemm()
                    r_value_turns(0)
                    r_scores()
                    r_value_turns(1)
                    h_gemm()
                    r_values()
                    h_gemm()
                    r_output_turns(0)
                    r_output_turns(1)
                    at.add("r")
                merge()
                project_merged()
                norm()
                at.add("norm")
                with at.loop(2, panel=PANELS_UP + PANELS_DOWN, acc=16, xb=2, half=1):
                    with at.loop(4, panel=4, acc=4):
                        gemm(m.h_hi, m.h_lo, fresh=True)
                        for _ in range(3):
                            h_gemm()
                    with at.loop(2, panel=8, xb=1):
                        project(m.up_hi, m.up_lo, 16, "up_ready", at.at("half", times=16) + 2)
                    at.add("half")

        @block.scalar
        def _(act):
            at = Place(act)
            activation = nc.scalar.activation

            def own(ins):
                ins.then_inc(s["act_step"], at.add("own"))
                act.wait_ge(s["act_step"], at.at("own"))

            def log_exp_tables():
                act.preload_act_table_set("natural_log_exp_and_others")

            def panel_done():
                act.wait_ge(s["used"], at.at("panel", RING + 1))
                at.add("panel")
                c = at.n.get("acc", 0) % 2
                at.add("acc")
                return c

            def skip_panel(accumulators=1):
                at.add("panel")
                at.add("acc", accumulators)

            def high_part(hi, ready, scale):
                c = panel_done()
                activation(hi[:], acc[c][:], ACT.Copy, scale=scale).then_inc(ready, 1)

            def copy_out(dst, ready):
                c = panel_done()
                own(activation(dst[:], acc[c][:], ACT.Copy))
                act.sem_inc(acc_free[c], 1)
                act.sem_inc(ready, 1)

            def inv_sqrt(dst, src, scale, eps, ready):
                own(activation(dst, src, ACT.Ln, bias=eps, scale=scale))
                activation(dst, dst, ACT.Exp, scale=-0.5).then_inc(ready, 1)

            def sums_of_squares():
                halves = m.x[:].rearrange("p b (c d) -> p b c d", c=2)
                for b in range(TB):
                    act.wait_ge(s["x_done"], at.at("proj", times=KT) + (b + 1))
                    ins = activation(m.junk[:, b], halves[:, b, 0], ACT.Square, accum_out=m.sm[:, b:b + 1])
                own(ins)
                own(activation(m.sm[:, 80:84], m.sm[:, 0:4], ACT.Identity, bias=m.col[:, 2:3], scale=1.0 / D))
                for b in range(TB):
                    act.wait_ge(s["x_done"], at.at("proj", times=KT) + (TB + b + 1))
                    own(activation(m.junk[:, b], halves[:, b, 1], ACT.Square, accum_out=m.sm[:, b:b + 1]))
                    inv_sqrt(m.sm[:, 4 + b:5 + b], m.sm[:, b:b + 1], 1.0 / D, m.sm[:, 80 + b:81 + b], s["rms_ready"])

            def norm(gain):
                act.dma_start(m.g_norm[:], gain).then_inc(s["gain_in"], 16)
                sums_of_squares()
                act.wait_ge(s["gain_in"], at.at("norm", 1, times=16))
                for k in range(KT):
                    act.wait_ge(s["xT_done"], at.at("norm", times=KT) + (k + 1))
                    activation(m.h_hi[:, k], xb[k % TB][:], ACT.Copy,
                               scale=m.g_norm[:, k:k + 1]).then_inc(s["h_hi_ready"], 1)
                at.add("norm")

            def of_layer(name, l):
                return t[name][bass.ds(l, 1)].squeeze(0)

            def layer_parameters(l):
                for dst, src in ((m.prm[:, 0:PRM_IN], of_layer("prm", l)),
                                 (m.prm[:, LAM_INIT:LAM_INIT + 1], t["lam_init"][bass.ds(l, 1)].to_broadcast([P, 1])),
                                 (m.lqk[:].rearrange("p a b -> p (a b)"),
                                  t["lambda_qk"][bass.ds(l, 1)].to_broadcast([P, 4 * A_DH])),
                                 (m.wif[:], of_layer("w_gates", l))):
                    act.dma_start(dst, src).then_inc(s["prm_in"], 16)

            def rotate_halves(dst, src, ready, half):
                for g in range(P // half):
                    act.dma_start(dst[half * g:half * g + half],
                                  src[half * (g ^ 1):half * (g ^ 1) + half]).then_inc(ready, 16)

            def qk_out(which, dst, sq_buf):
                c = panel_done()
                activation(sq_buf[:], acc[c][:], ACT.Square).then_inc(s["sq_ready"], 1)
                own(activation(dst[:], acc[c][:], ACT.Copy, scale=m.prm[:, G_QK + which:G_QK + which + 1]))
                act.sem_inc(acc_free[c], 1)

            def group_rstd(which, sq_buf, ahead):
                act.wait_ge(s["ss_done"], at.at("a", ahead, times=2) + (which + 1))
                own(activation(sq_buf[:], misc[:], ACT.Ln, bias=m.col[:, 2:3], scale=1.0 / A_DH))
                act.sem_inc(s["misc_free"], 1)
                activation(sq_buf[:], sq_buf[:], ACT.Exp, scale=-0.5).then_inc(s["rstd_ready"], 1)

            def values_out(ahead):
                act.wait_ge(s["vT_done"], at.at("a", ahead + 1))
                own(activation(m.v[:].rearrange("p b e -> p (b e)"), misc[:], ACT.Copy))
                act.sem_inc(s["misc_free"], 1)
                act.sem_inc(s["v_ready"], 1)

            def exponentials():
                act.wait_ge(s["pv_done"], at.at("a", 1))
                for j, qb in enumerate(order):
                    act.wait_ge(s["max_ready"], at.at("a", times=3) + (1, 2, 2, 3)[j])
                    for k, p in enumerate((m.p0, m.p1)):
                        i = 2 * j + k
                        ins = activation(p[:, QOFF[qb]:QOFF[qb] + (qb + 1) * P], sq[k][qb], ACT.Exp,
                                         bias=m.sm[:, 20 + i:21 + i], scale=A_DH ** -0.5,
                                         accum_out=m.sm[:, 28 + i:29 + i])
                    ins.then_inc(s["p_ready"], 1)

            def turned_out(g):
                act.wait_ge(s["turned"], at.at("a", times=len(groups)) + (g + 1))
                o = QOFF[groups[g][0]]
                activation(m.p1[:, o:o + turn[g].shape[-1]], turn[g], ACT.Copy).then_inc(s["aT_ready"], 1)

            def head_rstd():
                act.wait_ge(s["pv_done"], at.at("a", 2))
                for b in range(TB):
                    ins = activation(m.o_sq[:, b], pv[:, b * P:b * P + P], ACT.Square,
                                     scale=m.sm[:, 36 + 2 * b:37 + 2 * b], accum_out=m.sm[:, 48 + b:49 + b])
                own(ins)
                inv_sqrt(m.sm[:, 52:56], m.sm[:, 48:52], 1.0 / A_DV, m.col[:, 2:3], s["o_rstd_ready"])

            def sigmoid_out(dst, ready, free):
                c = panel_done()
                ins = activation(dst[:], acc[c][:], ACT.Sigmoid)
                if free:
                    own(ins)
                    act.sem_inc(acc_free[c], 1)
                    act.sem_inc(ready, 1)
                else:
                    ins.then_inc(ready, 1)

            def gate_rows():
                act.wait_ge(s["gates_done"], at.at("layer", 1))
                own(activation(m.g16[:], misc[0:16, :], ACT.Identity, bias=m.prm[0:16, BIASES:BIASES + 1]))
                act.sem_inc(s["misc_free"], 1)
                act.dma_start(m.frow[:], m.g16[8:16]).then_inc(s["f_in"], 16)
                act.wait_ge(s["f_in"], at.at("layer", 1, times=16))
                own(activation(m.lrow[:], m.frow[:], ACT.Abs))
                own(activation(m.lrow[:], m.lrow[:], ACT.Exp, scale=-1.0))
                activation(m.lrow[:], m.lrow[:], ACT.Ln, bias=m.col[0:8, 4:5]).then_inc(s["row_ln_ready"], 1)

            def gate_floor():
                act.wait_ge(s["rows_m_ready"], at.at("layer", 1))
                activation(m.erow[:], m.erow[:], ACT.Exp, scale=-1.0).then_inc(s["erow_ready"], 1)

            def m_sigmoid(src, dst, ready_src):
                act.wait_ge(ready_src, at.at("pair", 1))
                activation(dst[:], src[:], ACT.Sigmoid).then_inc(s["bsig_ready"], 1)

            def m_decays(a):
                act.wait_ge(s["gb_done"], at.at("pair", times=2) + (a + 1))
                act.wait_ge(s["pcol_ready"], at.at("pair", 1))
                for sb in range(TB):
                    bias, o = m.pcol[:, a, sb:sb + 1], SOFF[sb]
                    ins = activation(m.e[:, o:o + P], m.bank[3][:, sb * P:sb * P + P], ACT.Exp, bias=bias)
                    if sb < TB - 1:
                        ins = activation(m.e[:, o + P:o + S - sb * P], m.bank[2][:, (sb + 1) * P:S], ACT.Exp,
                                         bias=bias)
                ins.then_inc(s["e_ready"], 1)

            def m_values_out(a):
                act.wait_ge(s["bvT_done"], at.at("pair", times=2) + (a + 1))
                own(activation(m.va[a][:, :, 0:B_DV], misc[:].rearrange("p (b e) -> p b e", e=P), ACT.Copy))
                act.sem_inc(s["misc_free"], 1)
                act.sem_inc(s["bv_ready"], 1)

            def m_rstd(a):
                act.wait_ge(s["hs_ready"], at.at("pair", times=2) + (a + 2))
                for b in range(TB):
                    ins = activation(m.h_sq[:, b], m.hs[:, b], ACT.Square, accum_out=m.sm[:, 68 + b:69 + b])
                own(ins)
                inv_sqrt(m.sm[:, 72:76], m.sm[:, 68:72], 1.0 / B_DV, m.col[:, 2:3], s["b_rstd_ready"])

            def m_o_gate(a):
                act.wait_ge(s["gate_ready"], at.at("pair", times=2) + (a + 1))
                sigmoid_out(m.og, s["og_ready"], free=True)

            def softplus_parts(a):
                act.wait_ge(s["z_done"], at.at("r", times=2) + (a + 1))
                activation(m.sp[:, 0:512], m.bank[2][:], ACT.Abs)
                activation(m.sp[:, 512:1024], m.bank[3][:], ACT.Abs)
                own(activation(m.sp[:, 1024:1280], m.bank[4][:, 0:256], ACT.Abs))
                own(activation(m.sp[:], m.sp[:], ACT.Exp, scale=-1.0))
                activation(m.sp[:], m.sp[:], ACT.Ln, bias=m.col[:, 4:5]).then_inc(s["ln_ready"], 1)

            def stick_weights(a):
                act.wait_ge(s["c_done"], at.at("r", times=2) + (a + 1))
                activation(m.sp[:, 0:512], m.bank[2][:], ACT.Exp)
                activation(m.sp[:, 512:1024], m.bank[3][:], ACT.Exp)
                activation(m.sp[:, 1024:1280], m.bank[4][:, 0:256], ACT.Exp).then_inc(s["exp_ready"], 1)

            def s_values_out(a):
                act.wait_ge(s["svT_done"], at.at("r", times=2) + (a + 1))
                activation(m.sv_hi[:].rearrange("p b e -> p (b e)"), misc[:], ACT.Copy).then_inc(s["sv_hi_ready"], 1)

            def r_qk_out(dst):
                c = panel_done()
                own(activation(dst[:], acc[c][:], ACT.Copy))
                act.sem_inc(acc_free[c], 1)

            def r_values_out(half):
                act.wait_ge(s["rvT_done"], at.at("r", times=2) + (half + 1))
                activation(m.rv_hi[:, :, half * P:half * P + P], misc[:].rearrange("p (b e) -> p b e", e=P),
                           ACT.Copy).then_inc(s["rv_hi_ready"], 1)

            def merge():
                with at.loop(KT, panel=4, acc=4, u=1, own=2):
                    act.wait_ge(s["u_ready"], at.at("u", 1))
                    sigmoid_out(m.sig_a, s["sA_ready"], free=True)
                    skip_panel()
                    sigmoid_out(m.sig_b, s["sB_ready"], free=True)
                    skip_panel()
                    at.add("u")
                at.add("panel", PANELS_D)
                at.add("proj")

            cst = t["cst"]
            act.dma_start(m.posi[:], t["positions"].to_broadcast([P, S])).then_inc(s["pos_in"], 16)
            act.dma_start(m.ident[:], cst[:, C_IDENT:C_IDENT + P]).then_inc(s["const_in"], 16)
            act.dma_start(m.col[:], cst[:, C_INVF:C_INVF + 8]).then_inc(s["const_in"], 16)
            act.wait_ge(s["const_in"], 16 * 2)
            act.wait_ge(s["angles_ready"], 2)
            activation(m.sin[:], m.red[:], ACT.Sin)
            activation(m.cos[:], m.red2[:], ACT.Sin).then_inc(s["sin_ready"], 1)

            with at.loop(DEPTH, panel=PANELS_L1, acc=PANELS_L1 - PANELS_D, norm=1, proj=1, layer=1, a=A_HEADS,
                         pair=B_HEADS // 2, u=KT, own=ACT_L1) as l:
                log_exp_tables()
                act.wait_ge(s["x_done"], at.at("proj", times=KT) + 1)
                layer_parameters(l)
                norm(of_layer("norm_g", l))
                act.wait_ge(s["prm_in"], at.at("layer", 1, times=PRM_DMAS * 16))
                act.wait_ge(s["lam_sum"], at.at("layer", 1))
                activation(m.sm[:, 10:12], m.sm[:, 8:10], ACT.Exp).then_inc(s["lam_exp"], 1)
                qk_out(0, m.xq, m.sq_q)
                rotate_halves(m.rot_q, m.xq, s["rot_q_in"], 32)
                qk_out(1, m.xk, m.sq_k)
                rotate_halves(m.rot_k, m.xk, s["rot_k_in"], 32)
                group_rstd(0, m.sq_q, 0)
                copy_out(m.vT, s["vT_ready"])
                group_rstd(1, m.sq_k, 0)
                values_out(0)
                gate_rows()
                with at.loop(A_HEADS - 1, panel=4, acc=4, a=1, own=ACT_A):
                    log_exp_tables()
                    exponentials()
                    qk_out(0, m.xq, m.sq_q)
                    turned_out(0)
                    rotate_halves(m.rot_q, m.xq, s["rot_q_in"], 32)
                    qk_out(1, m.xk, m.sq_k)
                    rotate_halves(m.rot_k, m.xk, s["rot_k_in"], 32)
                    group_rstd(0, m.sq_q, 1)
                    turned_out(1)
                    turned_out(2)
                    copy_out(m.vT, s["vT_ready"])
                    group_rstd(1, m.sq_k, 1)
                    values_out(1)
                    head_rstd()
                    sigmoid_out(m.sg, s["sig_ready"], free=False)
                    at.add("a")
                log_exp_tables()
                exponentials()
                for g in range(len(groups)):
                    turned_out(g)
                head_rstd()
                gate_floor()
                sigmoid_out(m.sg, s["sig_ready"], free=False)
                at.add("a")
                at.add("layer")

                with at.loop(B_HEADS // 2, panel=8, acc=8, pair=1, own=ACT_B) as j:
                    act.dma_start(m.selp[:], t["sel"][:, bass.ds(j * 2, 2)]).then_inc(s["sel_in"], 16)
                    skip_panel()
                    m_sigmoid(m.yq, m.sgq, s["yq_ready"])
                    skip_panel()
                    m_sigmoid(m.yk, m.sgk, s["yk_ready"])
                    copy_out(m.vTb, s["bvT_ready"])
                    log_exp_tables()
                    m_decays(0)
                    m_values_out(0)
                    copy_out(m.vTb, s["bvT_ready"])
                    m_o_gate(0)
                    m_values_out(1)
                    sigmoid_out(m.zg, s["zg_ready"], free=False)
                    log_exp_tables()
                    m_decays(1)
                    m_rstd(0)
                    m_o_gate(1)
                    log_exp_tables()
                    m_rstd(1)
                    sigmoid_out(m.zg, s["zg_ready"], free=False)
                    at.add("pair")
                merge()

            act.wait_ge(s["x_done"], KT * DEPTH + 1)
            act.dma_start(m.cos[:], t["rot2"][:, 0]).then_inc(s["table_in"], 16)
            act.dma_start(m.sin[:], t["rot2"][:, 1]).then_inc(s["table_in"], 16)
            with at.loop(DEPTH, panel=PANELS_L2, acc=PANELS_L2 - PANELS_D - 2 * PANELS_DOWN, norm=2, proj=3,
                         r=R_HEADS, u=KT, up=32, own=ACT_L2) as l:
                log_exp_tables()
                norm(of_layer("g_mix_2", l))
                with at.loop(R_HEADS, panel=12, acc=12, r=1, own=ACT_R) as i:
                    log_exp_tables()
                    act.wait_ge(s["rw_ready"], at.at("r", 1))
                    act.dma_start(m.dec[:], t["decay"][:, bass.ds(i, 1)].squeeze(1)).then_inc(s["dec_in"], 16)
                    high_part(m.stq_hi, s["stq_ready"], S_DH ** -0.5)
                    high_part(m.stk_hi, s["sk_ready"], 1.0)
                    copy_out(m.svT, s["svT_ready"])
                    softplus_parts(0)
                    high_part(m.stq_hi, s["stq_ready"], S_DH ** -0.5)
                    s_values_out(0)
                    high_part(m.stk_hi, s["sk_ready"], 1.0)
                    stick_weights(0)
                    copy_out(m.svT, s["svT_ready"])
                    softplus_parts(1)
                    r_qk_out(m.rq)
                    rotate_halves(m.rrq, m.rq, s["rotq2_in"], 64)
                    s_values_out(1)
                    r_qk_out(m.rk)
                    stick_weights(1)
                    rotate_halves(m.rrk, m.rk, s["rotk2_in"], 64)
                    copy_out(m.rvT[0], s["rvT_ready"])
                    copy_out(m.rvT[1], s["rvT_ready"])
                    r_values_out(0)
                    r_values_out(1)
                    sigmoid_out(m.rg[0], s["rsig_ready"], free=False)
                    log_exp_tables()
                    act.wait_ge(s["var_ready"], at.at("r", 1))
                    inv_sqrt(m.sm[:, 64:68], m.sm[:, 56:64].rearrange("p (b k) -> p b k", k=2)[:, :, 1], 1.0,
                             m.col[:, 3:4], s["r_rstd_ready"])
                    sigmoid_out(m.rg[1], s["rsig_ready"], free=False)
                    at.add("r")
                merge()
                log_exp_tables()
                norm(of_layer("g_mlp_2", l))
                with at.loop(2, panel=PANELS_UP + PANELS_DOWN, acc=16, up=16, proj=1, own=16):
                    with at.loop(4, panel=4, acc=4, up=4, own=4):
                        for j in range(4):
                            c = panel_done()
                            act.wait_ge(s["up_ready"], at.at("up", 1))
                            own(activation(m.m[j % 2][:], acc[c][:], ACT.Relu))
                            act.sem_inc(acc_free[c], 1)
                            activation(m.mm[j % 2][:], m.m[j % 2][:], ACT.Square).then_inc(s["up_sq_ready"], 1)
                            at.add("up")
                    at.add("panel", PANELS_DOWN)
                    at.add("proj")
            log_exp_tables()
            act.wait_ge(s["x_done"], at.at("proj", times=KT) + 1)
            act.dma_start(m.g_fin[:], t["g_final_2"].rearrange("(a d) -> a d", a=1).to_broadcast([P, D])
                          ).then_inc(s["gfin_in"], 16)
            sums_of_squares()

        @block.vector
        def _(dve):
            at = Place(dve)
            tt, ts, stt = nc.vector.tensor_tensor, nc.vector.tensor_scalar, nc.vector.scalar_tensor_tensor
            for name, credit in (("acc_free0", 1), ("acc_free1", 1), ("misc_free", 1), ("on_ready", 1), ("hs_ready", 1),
                                 ("u_ready", 1), ("up_ready", 2), ("rw_ready", 1), ("gate_ready", 1), ("so_free", 1),
                                 ("bank2_free", 1)):
                dve.sem_inc(s[name], credit)

            def own(ins):
                ins.then_inc(s["dve_step"], at.add("own"))
                dve.wait_ge(s["dve_step"], at.at("own"))

            def panel_done():
                dve.wait_ge(s["used"], at.at("panel", RING + 1))
                return take_panel()

            def take_panel():
                at.add("panel")
                c = at.n.get("acc", 0) % 2
                at.add("acc")
                return c

            def split(hi, lo, src, ready):
                own(ts(hi, src, 1.0, None, ALU.mult))
                tt(lo, src, hi.bitcast(F32), ALU.subtract).then_inc(ready, 1)

            def tile(buf, k):
                return buf[:, bass.ds(k, 1)].squeeze(1) if not isinstance(k, int) else buf[:, k]

            def norm():
                for b in range(TB):
                    dve.wait_ge(s["rms_ready"], at.at("norm", times=TB) + (b + 1))
                    ts(m.xn[:, b], m.x[:, b], m.sm[:, 4 + b:5 + b], None, ALU.mult).then_inc(s["xn_ready"], 1)
                for k in range(KT):
                    dve.wait_ge(s["h_hi_ready"], at.at("norm", times=KT) + (k + 1))
                    stt(m.h_lo[:, k], xb[k % TB][:], m.g_norm[:, k:k + 1], m.h_hi[:, k].bitcast(F32), ALU.mult,
                        ALU.subtract).then_inc(s["h_ready"], 1)
                at.add("norm")

            def add_to_x(tiles):
                with at.loop(2, panel=tiles // 2, proj4=1) as c:
                    at.add("panel", tiles // 2)
                    for b in range(TB):
                        if b < TB - 1:
                            dve.wait_ge(s["xb_done"], at.at("proj4", times=TB - 1) + (b + 1))
                        else:
                            dve.wait_ge(s["used"], at.at("panel", RING))
                        xs = m.x[:, b, bass.ds(c * 512, 512)]
                        tt(xs, xs, xb[b][:], ALU.add).then_inc(s["x_done"], 1)
                    at.add("proj4")

            def lambdas():
                dve.wait_ge(s["prm_in"], at.at("layer", 1, times=PRM_DMAS * 16))
                own(ts(m.wif_hi[:], m.wif[:], 1.0, None, ALU.mult))
                tt(m.wif_lo[:], m.wif[:], m.wif_hi[:].bitcast(F32), ALU.subtract).then_inc(s["wif_ready"], 1)
                own(tt(m.lqp[:], m.lqk[:].rearrange("p (a two) d -> p a two d", two=2)[:, :, 0],
                       m.lqk[:].rearrange("p (a two) d -> p a two d", two=2)[:, :, 1], ALU.mult))
                nc.vector.tensor_reduce(m.sm[:, 8:10], m.lqp[:], AX_X, ALU.add).then_inc(s["lam_sum"], 1)
                lam_init, gain = m.prm[:, LAM_INIT:LAM_INIT + 1], m.prm[:, G_A_SCALED:G_A_SCALED + 1]
                neg_lambda = m.prm[:, NEG_LAMBDA:NEG_LAMBDA + 1]
                own(ts(gain, lam_init, -1.0, 1.0, ALU.mult, ALU.add))
                own(tt(gain, gain, m.prm[:, G_A:G_A + 1], ALU.mult))
                nc.vector.memset(m.zrow[:], 0.0).then_inc(s["dve_step"], at.add("own"))
                dve.wait_ge(s["lam_exp"], at.at("layer", 1))
                own(tt(neg_lambda, m.sm[:, 11:12], m.sm[:, 10:11], ALU.subtract))
                own(tt(neg_lambda, neg_lambda, lam_init, ALU.subtract))

            def gate_rows():
                dve.wait_ge(s["row_ln_ready"], at.at("layer", 1))
                own(ts(m.fcum[:], m.frow[:], 0.0, None, ALU.min))
                own(tt(m.fcum[:], m.fcum[:], m.lrow[:], ALU.subtract))
                own(nc.vector.tensor_tensor_scan(m.frow[:], m.fcum[:], m.zrow[:], 0.0, ALU.add, ALU.add))
                own(tt(m.grow[:], m.g16[0:8], m.frow[:], ALU.subtract))
                own(nc.vector.tensor_tensor_scan(m.erow[:], m.grow[:], m.grow[:], BIG_NEG, ALU.max, ALU.max))
                own(ts(m.negg[:], m.erow[:], -1.0, None, ALU.mult))
                split(m.negg_hi[:], m.negg_lo[:], m.negg[:], s["rows_ready"])
                tt(m.erow[:], m.erow[:], m.frow[:], ALU.add).then_inc(s["rows_m_ready"], 1)

            def rotate(x, rot, cos, sin, rstd):
                tt(x[:], x[:], cos[:], ALU.mult)
                own(tt(rot[:], rot[:], sin[:], ALU.mult))
                ins = tt(x[:], x[:], rot[:], ALU.add)
                if rstd is not None:
                    own(ins)
                    dve.wait_ge(*rstd[1])
                    ins = tt(x[:], x[:], rstd[0][:], ALU.mult)
                own(ins)

            def split_squares(which, ahead):
                dve.wait_ge(s["sq_ready"], at.at("a", ahead, times=2) + (which + 1))
                hi, lo, sq_buf = ((m.sqh_q, m.sql_q, m.sq_q), (m.sqh_k, m.sql_k, m.sq_k))[which]
                split(hi[:], lo[:], sq_buf[:], s["sq_split"])

            def rotate_qk(which, ahead):
                x, rot, sqb = ((m.xq, m.rot_q, m.sq_q), (m.xk, m.rot_k, m.sq_k))[which]
                dve.wait_ge(s["rot_k_in" if which else "rot_q_in"], at.at("a", ahead + 1, times=64))
                rotate(x, rot, m.cos, m.sin,
                       (sqb, (s["rstd_ready"], at.at("a", ahead, times=2) + (which + 1))))
                hi, lo = ((m.q_hi, m.q_lo), (m.k_hi, m.k_lo))[which]
                split(hi[:], lo[:], x[:], s["qk_ready"])

            def maxima(banks):
                for i in banks:
                    for k in range(2):
                        ins = nc.vector.tensor_reduce(m.sm[:, 12 + 2 * i + k:13 + 2 * i + k], sq[k][order[i]],
                                                      AX_X, ALU.max)
                own(ins)
                w = slice(2 * banks[0], 2 * banks[-1] + 2)
                ts(m.sm[:, 20:28][:, w], m.sm[:, 12:20][:, w], -(A_DH ** -0.5), None,
                   ALU.mult).then_inc(s["max_ready"], 1)

            def combine(i):
                qb = order[i]
                dve.wait_ge(s["p_ready"], at.at("a", times=TB) + (i + 1))
                l0, ratio = m.sm[:, 28 + 2 * i:29 + 2 * i], m.sm[:, 44 + i:45 + i]
                own(nc.vector.reciprocal(m.sm[:, 36 + 2 * qb:38 + 2 * qb], m.sm[:, 28 + 2 * i:30 + 2 * i]))
                own(stt(ratio, l0, m.prm[:, NEG_LAMBDA:NEG_LAMBDA + 1], m.sm[:, 37 + 2 * qb:38 + 2 * qb],
                        ALU.mult, ALU.mult))
                w = slice(QOFF[qb], QOFF[qb] + (qb + 1) * P)
                stt(m.p0[:, w], m.p1[:, w], ratio, m.p0[:, w], ALU.mult, ALU.add).then_inc(s["a_ready"], 1)

            def weights():
                dve.wait_ge(s["scores_done"], at.at("a", 1, times=2))
                maxima((0,))
                maxima((1, 2))
                combine(0)
                combine(1)
                maxima((3,))
                combine(2)
                combine(3)

            def head_normalised():
                dve.wait_ge(s["o_rstd_ready"], at.at("a", 1))
                own(tt(m.sm[:, 56:60].unsqueeze(2), m.sm[:, 52:56].unsqueeze(2),
                       m.sm[:, 36:44].rearrange("p (b k) -> p b k", k=2)[:, :, 0:1], ALU.mult))
                tt(m.o_sb[:], pv[:].rearrange("p (b e) -> p b e", e=P),
                   m.sm[:, 56:60].unsqueeze(2).to_broadcast([P, TB, P]), ALU.mult).then_inc(s["on_ready"], 1)

            def head_gate():
                dve.wait_ge(s["sig_ready"], at.at("a", 1))
                c = take_panel()
                own(tt(m.sz[:], acc[c][:], m.sg[:], ALU.mult))
                dve.sem_inc(acc_free[c], 1)

            def head_branch(k):
                dve.wait_ge(s["oT_done"], at.at("a", 1))
                own(stt(m.sz[:], misc[:], m.prm[:, G_A_SCALED:G_A_SCALED + 1], m.sz[:], ALU.mult, ALU.mult))
                dve.sem_inc(s["misc_free"], 1)
                split(tile(m.a_hi, k), tile(m.a_lo, k), m.sz[:], s["branch_a"])

            def convolve(y, kt, ready):
                c = panel_done()
                a = acc[c]
                w = [m.prm[:, bass.ds(kt + (CONV_W + KT * tap), 1)] for tap in range(A_TAPS)]
                own(ts(y[:], a[:], w[A_TAPS - 1], m.prm[:, bass.ds(kt + CONV_B, 1)], ALU.mult, ALU.add))
                for tap in range(A_TAPS - 2, -1, -1):
                    d = A_TAPS - 1 - tap
                    own(stt(y[:, d:], a[:, :S - d], w[tap], y[:, d:], ALU.mult, ALU.add))
                dve.sem_inc(acc_free[c], 1)
                dve.sem_inc(ready, 1)

            def m_weights(a):
                dve.wait_ge(s["e_ready"], at.at("pair", times=2) + (a + 1))
                dve.wait_ge(s["bs_done"], at.at("pair", times=2) + (a + 1))
                for sb in range(TB):
                    w = slice(SOFF[sb], SOFF[sb] + S - sb * P)
                    ins = tt(m.e[:, w], mst[sb], m.e[:, w], ALU.mult)
                ins.then_inc(s["bw_ready"], 1)

            def m_output(j, a):
                dve.wait_ge(s["bpv_done"], at.at("pair", times=2) + (a + 1))
                outs = [m.bank[2 + k][:, 0:2 * (B_DV + 4)].rearrange("p (b e) -> p b e", e=B_DV + 4) for k in range(2)]
                den, mag = m.sm[:, 56:60], m.sm[:, 60:64]
                for k in range(2):
                    ins = nc.vector.tensor_copy(den[:, 2 * k:2 * k + 2], outs[k][:, :, B_DV])
                own(ins)
                own(stt(mag, den, -1.0, den, ALU.mult, ALU.max))
                own(tt(mag, mag, m.ecol[:, bass.ds(j * 2 + a, 1)].squeeze(1), ALU.max))
                own(nc.vector.reciprocal(den, mag))
                for k in range(2):
                    ins = tt(m.hs[:, 2 * k:2 * k + 2], outs[k][:, :, 0:B_DV],
                             den[:, 2 * k:2 * k + 2].unsqueeze(2).to_broadcast([P, 2, B_DV]), ALU.mult)
                ins.then_inc(s["hs_ready"], 1)

            def m_normalised(a):
                dve.wait_ge(s["b_rstd_ready"], at.at("pair", times=2) + (a + 1))
                tt(m.hs[:], m.hs[:], m.sm[:, 72:76].unsqueeze(2).to_broadcast([P, TB, B_DV]),
                   ALU.mult).then_inc(s["bon_ready"], 1)

            def m_gate(a):
                dve.wait_ge(s["zg_ready"], at.at("pair", times=2) + (a + 1))
                take_panel()
                c = take_panel()
                own(tt(m.gate[:], acc[c][:], m.zg[:], ALU.mult))
                dve.sem_inc(acc_free[c], 1)
                dve.wait_ge(s["og_ready"], at.at("pair", times=2) + (a + 1))
                own(tt(m.gate[:], m.gate[:], m.og[:], ALU.mult))
                dve.sem_inc(s["gate_ready"], 1)

            def m_branch(j, a):
                dve.wait_ge(s["boT_done"], at.at("pair", times=2) + (a + 1))
                own(stt(m.gate[:], misc[:], m.prm[:, G_B:G_B + 1], m.gate[:], ALU.mult, ALU.mult))
                dve.sem_inc(s["misc_free"], 1)
                split(tile(m.b_hi, j * 2 + a), tile(m.b_lo, j * 2 + a), m.gate[:], s["branch_b"])

            def merge():
                with at.loop(KT, panel=4, acc=4, u=1, own=4) as n:
                    dve.wait_ge(s["sA_ready"], at.at("u", 1))
                    take_panel()
                    c = panel_done()
                    own(tt(m.sig_a[:], acc[c][:], m.sig_a[:], ALU.mult))
                    dve.sem_inc(acc_free[c], 1)
                    dve.wait_ge(s["sB_ready"], at.at("u", 1))
                    take_panel()
                    c = panel_done()
                    own(tt(m.sig_b[:], acc[c][:], m.sig_b[:], ALU.mult))
                    dve.sem_inc(acc_free[c], 1)
                    own(tt(m.sig_a[:], m.sig_a[:], m.sig_b[:], ALU.add))
                    split(tile(m.u_hi, n), tile(m.u_lo, n), m.sig_a[:], s["u_ready"])
                    at.add("u")

            def stick_low_parts(a):
                for hi, lo, scale, ready in ((m.stq_hi, m.stq_lo, S_DH ** -0.5, s["stq_ready"]),
                                             (m.stk_hi, m.stk_lo, 1.0, s["sk_ready"])):
                    dve.wait_ge(ready, at.at("r", times=2) + (a + 1))
                    c = take_panel()
                    own(stt(lo[:], acc[c][:], scale, hi[:].bitcast(F32), ALU.mult, ALU.subtract))
                    dve.sem_inc(acc_free[c], 1)
                dve.sem_inc(s["sk_lo_ready"], 1)
                take_panel()

            def softplus(a):
                dve.wait_ge(s["ln_ready"], at.at("r", times=2) + (a + 1))
                for i, n in enumerate((512, 512, 256)):
                    w = slice(512 * i, 512 * i + n)
                    ins = stt(m.sp[:, w], m.bank[2 + i][:, 0:n], 0.0, m.sp[:, w], ALU.max, ALU.add)
                own(ins)
                split(m.sp_hi[:], m.sp_lo[:], m.sp[:], s["sp_ready"])

            def stick_values_low(a):
                dve.wait_ge(s["sv_hi_ready"], at.at("r", times=2) + (a + 1))
                own(tt(m.sv_lo[:].rearrange("p b e -> p (b e)"), misc[:],
                       m.sv_hi[:].rearrange("p b e -> p (b e)").bitcast(F32), ALU.subtract))
                dve.sem_inc(s["misc_free"], 1)
                dve.sem_inc(s["sv_ready"], 1)

            def stick_weights_split(a):
                dve.wait_ge(s["exp_ready"], at.at("r", times=2) + (a + 1))
                split(m.sw_hi[:], m.sp_lo[:], m.sp[:], s["sw_ready"])

            def r_values_low(half):
                dve.wait_ge(s["rv_hi_ready"], at.at("r", times=2) + (half + 1))
                w = slice(half * P, half * P + P)
                own(tt(m.rv_lo[:, :, w], misc[:].rearrange("p (b e) -> p b e", e=P),
                       m.rv_hi[:, :, w].bitcast(F32), ALU.subtract))
                dve.sem_inc(s["misc_free"], 1)
                dve.sem_inc(s["rv_ready"], 1)

            def stick_branch(i, a):
                dve.wait_ge(s["so_done"], at.at("r", times=2) + (a + 1))
                hi, lo = tile(m.b_hi, i * 2 + a), tile(m.b_lo, i * 2 + a)
                own(ts(hi, m.bank[5][:], 1.0, None, ALU.mult))
                own(tt(lo, m.bank[5][:], hi.bitcast(F32), ALU.subtract))
                dve.sem_inc(s["so_free"], 1)
                dve.sem_inc(s["branch_b"], 1)

            def r_weights():
                dve.wait_ge(s["rs_done"], at.at("r", 1))
                dve.wait_ge(s["dec_in"], at.at("r", 1, times=16))
                for sb in range(TB):
                    n = S - sb * P
                    ins = tt(m.sp[:, SOFF[sb]:SOFF[sb] + n], st[sb], m.dec[:, 0:n], ALU.mult)
                own(ins)
                split(m.sw_hi[:], m.sp_lo[:], m.sp[:], s["rw_ready"])

            def r_statistics():
                dve.wait_ge(s["rpv_done"], at.at("r", 1))
                for b in range(TB):
                    ins = nc.vector.bn_stats(m.sm[:, 12 + 6 * b:18 + 6 * b],
                                             m.bank[5 + b // 2][:, (b % 2) * R_DV:(b % 2) * R_DV + R_DV])
                own(ins)
                dve.sem_inc(s["stats_step"], 1)
                for b in range(TB):
                    ins = nc.vector.bn_aggr(m.sm[:, 56 + 2 * b:58 + 2 * b], m.sm[:, 12 + 6 * b:18 + 6 * b])
                ins.then_inc(s["var_ready"], 1)

            def r_normalised():
                dve.wait_ge(s["r_rstd_ready"], at.at("r", 1))
                for b in range(TB):
                    ins = ts(m.ro[:, b], m.bank[5 + b // 2][:, (b % 2) * R_DV:(b % 2) * R_DV + R_DV],
                             m.sm[:, 56 + 2 * b:57 + 2 * b], m.sm[:, 64 + b:65 + b], ALU.subtract, ALU.mult)
                ins.then_inc(s["ro_ready"], 1)

            def r_gate(half):
                dve.wait_ge(s["rsig_ready"], at.at("r", times=2) + (half + 1))
                c = take_panel()
                own(tt(m.rg[half][:], acc[c][:], m.rg[half][:], ALU.mult))
                dve.sem_inc(acc_free[c], 1)

            def r_branch(i, half):
                dve.wait_ge(s["roT_done"], at.at("r", times=2) + (half + 1))
                own(tt(m.rg[half][:], (misc, m.bank[2])[half][:], m.rg[half][:], ALU.mult))
                dve.sem_inc(s[("misc_free", "bank2_free")[half]], 1)
                split(tile(m.a_hi, i * 2 + half), tile(m.a_lo, i * 2 + half), m.rg[half][:], s["branch_a"])

            dve.wait_ge(s["const_in"], 16 * 2)
            dve.wait_ge(s["pos_in"], 16)
            own(nc.vector.tensor_copy(m.ang[:], m.posi[:]))
            own(ts(m.ang[:], m.ang[:], m.col[:, 0:1], None, ALU.mult))
            own(ts(m.turns[:], m.ang[:], 1.0 / (2 * math.pi), None, ALU.mult))
            own(nc.vector.tensor_copy(m.turni[:], m.turns[:]))
            own(nc.vector.tensor_copy(m.turns[:], m.turni[:]))
            own(stt(m.red[:], m.turns[:], -TWO_PI[0], m.ang[:], ALU.mult, ALU.add))
            own(stt(m.red[:], m.turns[:], -TWO_PI[1], m.red[:], ALU.mult, ALU.add))
            own(stt(m.red[:], m.turns[:], -TWO_PI[2], m.red[:], ALU.mult, ALU.add))

            def wrap(x):
                own(ts(m.turns[:], x[:], math.pi, -2 * math.pi, ALU.is_gt, ALU.mult))
                own(tt(x[:], x[:], m.turns[:], ALU.add))
                own(ts(m.turns[:], x[:], -math.pi, 2 * math.pi, ALU.is_lt, ALU.mult))
                own(tt(x[:], x[:], m.turns[:], ALU.add))

            wrap(m.red)
            own(ts(m.red2[:], m.red[:], math.pi / 2, None, ALU.add))
            wrap(m.red2)
            for x in (m.red, m.red2):
                ts(x[:], x[:], SIN_MAX, -SIN_MAX, ALU.min, ALU.max).then_inc(s["angles_ready"], 1)
            dve.wait_ge(s["sin_ready"], 1)
            own(ts(m.sin[:], m.sin[:], m.col[:, 1:2], None, ALU.mult))
            for b in range(TB):
                dve.wait_ge(x_in[b], 16)
                dve.sem_inc(s["x_done"], 1)
            dve.sem_inc(s["x_done"], TB)
            dve.wait_ge(s["mask_in"], 16)
            for dst, src in ((m.ident_b, m.ident[:]), (m.mq_b, m.cst[:, C_MQ:C_MQ + P]),
                             (m.ms_b, m.cst[:, C_MS:C_MS + TB * P]), (m.mx_b, m.cst[:, C_MX:C_MX + P])):
                nc.vector.tensor_copy(dst[:], src).then_inc(s["masks_ready"], 1)
            for dst, c in ((m.ntri, C_TRI), (m.neg1, C_NEG1), (m.grp, C_GRP)):
                ts(dst[:], m.cst[:, c:c + P], 1.0, None, ALU.mult).then_inc(s["masks_ready"], 1)

            with at.loop(DEPTH, panel=PANELS_L1, acc=PANELS_L1 - PANELS_D, norm=1, proj4=2, layer=1, a=A_HEADS,
                         pair=B_HEADS // 2, u=KT, own=DVE_L1):
                norm()
                lambdas()
                take_panel()
                take_panel()
                take_panel()
                split_squares(0, 0)
                split_squares(1, 0)
                rotate_qk(0, 0)
                rotate_qk(1, 0)
                with at.loop(A_HEADS - 1, panel=4, acc=4, a=1, own=DVE_A) as i:
                    weights()
                    take_panel()
                    take_panel()
                    take_panel()
                    split_squares(0, 1)
                    split_squares(1, 1)
                    rotate_qk(0, 1)
                    rotate_qk(1, 1)
                    head_normalised()
                    head_gate()
                    head_branch(i)
                    at.add("a")
                weights()
                gate_rows()
                head_normalised()
                dve.wait_ge(s["rowsT_done"], at.at("layer", 1))
                cols_ps = misc[:, 0:64].rearrange("p (i b h) -> p i h b", i=2, h=B_HEADS)
                nc.vector.tensor_copy(m.gcol[:], cols_ps[:, 0])
                own(nc.vector.tensor_copy(m.ecol[:], cols_ps[:, 1]))
                dve.sem_inc(s["misc_free"], 1)
                head_gate()
                head_branch(A_HEADS - 1)
                at.add("a")
                for va in m.va:
                    nc.vector.memset(va[:, :, B_DV:B_DV + 1], 1.0)
                at.add("layer")

                with at.loop(B_HEADS // 2, panel=8, acc=8, pair=1, own=DVE_B) as j:
                    dve.wait_ge(s["sel_in"], at.at("pair", 1, times=16))
                    ts(m.selp_r[:], m.selp[:], 1.0, None, ALU.mult).then_inc(s["sel_ready"], 1)
                    ts(m.pcol[:], m.gcol[:, bass.ds(j * 2, 2)], 1.0, None, ALU.mult).then_inc(s["pcol_ready"], 1)
                    convolve(m.yq, j, s["yq_ready"])
                    convolve(m.yk, j + 4, s["yk_ready"])
                    take_panel()
                    take_panel()
                    dve.wait_ge(s["bsig_ready"], at.at("pair", times=2) + 1)
                    own(stt(m.yq[:], m.yq[:], B_DK ** -0.5, m.sgq[:], ALU.mult, ALU.mult))
                    dve.wait_ge(s["bsig_ready"], at.at("pair", times=2) + 2)
                    own(tt(m.yk[:], m.yk[:], m.sgk[:], ALU.mult))
                    split(m.yq_hi[:], m.yq_lo[:], m.yq[:], s["bqk_ready"])
                    split(m.yk_hi[:], m.yk_lo[:], m.yk[:], s["bqk_ready"])
                    m_weights(0)
                    m_gate(0)
                    m_output(j, 0)
                    m_weights(1)
                    m_normalised(0)
                    m_branch(j, 0)
                    m_output(j, 1)
                    m_normalised(1)
                    m_gate(1)
                    m_branch(j, 1)
                    at.add("pair")
                merge()
                add_to_x(KT)

            with at.loop(DEPTH, panel=PANELS_L2, acc=PANELS_L2 - PANELS_D - 2 * PANELS_DOWN, norm=2, proj4=6,
                         r=R_HEADS, u=KT, up=32, own=DVE_L2):
                norm()
                with at.loop(R_HEADS, panel=12, acc=12, r=1, own=DVE_R) as i:
                    stick_low_parts(0)
                    softplus(0)
                    stick_values_low(0)
                    stick_low_parts(1)
                    stick_weights_split(0)
                    stick_branch(i, 0)
                    softplus(1)
                    stick_values_low(1)
                    at.add("panel", 4)
                    at.add("acc", 4)
                    dve.wait_ge(s["rotq2_in"], at.at("r", 1, times=32))
                    dve.wait_ge(s["table_in"], 32)
                    rotate(m.rq, m.rrq, m.cos, m.sin, None)
                    split(m.rq_hi[:], m.rq_lo[:], m.rq[:], s["rqk_ready"])
                    stick_weights_split(1)
                    dve.wait_ge(s["rotk2_in"], at.at("r", 1, times=32))
                    rotate(m.rk, m.rrk, m.cos, m.sin, None)
                    split(m.rk_hi[:], m.rk_lo[:], m.rk[:], s["rqk_ready"])
                    stick_branch(i, 1)
                    r_values_low(0)
                    r_weights()
                    r_values_low(1)
                    r_gate(0)
                    r_statistics()
                    r_normalised()
                    r_gate(1)
                    r_branch(i, 0)
                    r_branch(i, 1)
                    at.add("r")
                merge()
                add_to_x(KT)
                norm()
                with at.loop(2, panel=PANELS_UP + PANELS_DOWN, acc=16, up=16, proj4=2, own=16) as f:
                    with at.loop(4, panel=4, acc=4, up=4, own=4) as n:
                        for j in range(4):
                            dve.wait_ge(s["up_sq_ready"], at.at("up", 1))
                            take_panel()
                            split(tile(m.up_hi, n * 4 + j), tile(m.up_lo, n * 4 + j), m.mm[j % 2][:], s["up_ready"])
                            at.add("up")
                    add_to_x(16)
            dve.wait_ge(s["gfin_in"], 16)
            for b in range(TB):
                dve.wait_ge(s["rms_ready"], at.at("norm", times=TB) + (b + 1))
                stt(m.xn[:, b], m.x[:, b], m.sm[:, 4 + b:5 + b], m.g_fin[:], ALU.mult,
                    ALU.mult).then_inc(s["out_ready"], 1)


def lay_out(inputs):
    a = {name: np.asarray(value) for name, value in inputs.items()}
    t = {name: a[name] for name in ("x", "positions", "g_final_2")}

    def columns(w):
        return w.reshape(DEPTH, KT, P, -1, P).transpose(0, 3, 2, 1, 4).reshape(DEPTH, -1, P, D)

    def rows(w):
        return w.reshape(DEPTH, -1, 2, P, 2, 512).transpose(0, 4, 1, 3, 2, 5).reshape(DEPTH, -1, P, D)

    def by_partition(v):
        return v.reshape(DEPTH, -1, P).transpose(0, 2, 1)

    w_in = a["w_in"]
    gates = slice(GATES, GATES + 2 * B_HEADS)
    t["w_in"] = columns(np.concatenate([w_in[:, :, :gates.start], w_in[:, :, gates.stop:]], 2))
    t["w_gates"] = w_in[:, :, gates].reshape(DEPTH, KT, P, -1).transpose(0, 2, 1, 3)
    for name in ("w_in_2", "w_out_a", "w_out_b", "p_ret_2", "p_sb_2", "w_up_2"):
        t[name] = columns(a[name])
    for name in ("w_o", "w_out_2", "w_down_2"):
        t[name] = rows(a[name])
    for name in ("norm_g", "g_mix_2", "g_mlp_2"):
        t[name] = by_partition(a[name])
    t["lambda_qk"] = a["lambda_qk"].reshape(DEPTH, -1)
    biases = np.zeros((DEPTH, P), np.float32)
    biases[:, :2 * B_HEADS] = np.concatenate([a["igate_b"], a["fgate_b"]], 1)
    t["prm"] = np.concatenate(
        [by_partition(v) for v in (np.tile(a["q_norm_g"], 2), np.tile(a["k_norm_g"], 2), a["mlstm_norm_g"], biases,
                                   a["attn_norm_g"], a["conv_w"].reshape(DEPTH, -1), a["conv_b"])], 2)
    return t


def kernel(**inputs):
    import concourse.bacc as bacc
    from concourse.bass_utils import run_bass_kernel_spmd

    nc = bacc.Bacc("TRN2", target_bir_lowering=False, num_devices=1)
    arrays, t = {}, {}
    for name, a in {**lay_out(inputs), **constant_arrays()}.items():
        a = np.ascontiguousarray(a)
        arrays[f"in_{name}"] = a
        t[name] = nc.dram_tensor(f"in_{name}", a.shape, mybir.dt.from_np(a.dtype), kind="ExternalInput").ap()
    out = nc.dram_tensor("out_x", (1, S, D), F32, kind="ExternalOutput").ap()
    program(nc, t, out)
    r = run_bass_kernel_spmd(nc, [arrays], core_ids=[0])
    return r.results[0]["out_x"]
```
